# Optimizing a Trainium2 kernel written in Bass

```python
import math
import jax, jax.numpy as jnp
from jax import lax
import numpy as np

D_MODEL = 1024
BATCH = 1
SEQ = 256
DEPTH = 4

N_MIXERS = 4
EPS = 1e-6
NEG = -1e30
MLSTM_HEADS = 4
MLSTM_DQK = 128
MLSTM_DV = D_MODEL // MLSTM_HEADS
MLSTM_CHUNK = 128
MLSTM_IN = 2 * MLSTM_HEADS * MLSTM_DQK + 2 * MLSTM_HEADS * MLSTM_DV + 2 * MLSTM_HEADS
ATTN_HEADS = 16
ATTN_DH = D_MODEL // ATTN_HEADS
ROPE_DIMS = ATTN_DH // 4
ROPE_THETA = 500000.0
MOBA_BLOCK = 256
MOBA_TOPK = 3
Q_BLOCK = 128
CONV_WIDTH = 3
FFN_HIDDEN = -(-(8 * D_MODEL) // (3 * 256)) * 256

kernel_name = "hybrid_mlstm_moba_shortconv_stickbreak"

def rms_norm(x, g):
    xf = x.astype(jnp.float32)
    y = xf * lax.rsqrt(jnp.mean(xf * xf, axis=-1, keepdims=True) + EPS)
    return (y * g.astype(jnp.float32)).astype(x.dtype)

def partial_rope(x, positions):
    half = ROPE_DIMS // 2
    inv = ROPE_THETA ** (-jnp.arange(half, dtype=jnp.float32) / half)
    ang = positions.astype(jnp.float32)[..., None] * inv
    cos = jnp.cos(ang)[:, :, None, :]
    sin = jnp.sin(ang)[:, :, None, :]
    xr = x[..., :ROPE_DIMS].astype(jnp.float32)
    x1, x2 = xr[..., :half], xr[..., half:]
    rot = jnp.concatenate([x1 * cos - x2 * sin, x2 * cos + x1 * sin], axis=-1).astype(x.dtype)
    return jnp.concatenate([rot, x[..., ROPE_DIMS:]], axis=-1)

def mlstm_mixer(h, w_in, b_gate, head_gain, w_out):
    B, S, _ = h.shape
    NH, DK, DV, L = MLSTM_HEADS, MLSTM_DQK, MLSTM_DV, MLSTM_CHUNK
    nc = S // L
    proj = h @ w_in
    q, k, v, o_pre, g_pre = jnp.split(
        proj, [NH * DK, 2 * NH * DK, 2 * NH * DK + NH * DV, 2 * NH * DK + 2 * NH * DV], axis=-1)
    g = g_pre.astype(jnp.float32) + b_gate.astype(jnp.float32)
    i_log = g[..., :NH]
    f_log = jax.nn.log_sigmoid(g[..., NH:])

    def to_chunks(t, d):
        return t.astype(jnp.float32).reshape(B, nc, L, NH, d).transpose(1, 0, 3, 2, 4)

    def gate_chunks(t):
        return t.reshape(B, nc, L, NH).transpose(1, 0, 3, 2)

    qc = to_chunks(q, DK) * (DK ** -0.5)
    kc = to_chunks(k, DK)
    vc = to_chunks(v, DV)
    ic = gate_chunks(i_log)
    fc = gate_chunks(f_log)
    causal = jnp.tril(jnp.ones((L, L), dtype=bool))

    def step(carry, xs):
        C, n, m = carry
        q_, k_, v_, i_, f_ = xs
        b = jnp.cumsum(f_, axis=-1)
        dmat = jnp.where(causal, b[..., :, None] - b[..., None, :] + i_[..., None, :], -jnp.inf)
        inter = b + m[..., None]
        m_t = jnp.maximum(inter, jnp.max(dmat, axis=-1))
        w_intra = jnp.exp(dmat - m_t[..., None])
        w_inter = jnp.exp(inter - m_t)
        s = jnp.einsum('bhtd,bhsd->bhts', q_, k_) * w_intra
        num = jnp.einsum('bhts,bhsv->bhtv', s, v_) + w_inter[..., None] * jnp.einsum('bhtd,bhdv->bhtv', q_, C)
        den = jnp.sum(s, axis=-1) + w_inter * jnp.einsum('bhtd,bhd->bht', q_, n)
        den = jnp.maximum(jnp.abs(den), jnp.exp(-m_t))
        h_out = num / den[..., None]
        g_tot = b[..., -1]
        a = g_tot[..., None] - b + i_
        m_new = jnp.maximum(g_tot + m, jnp.max(a, axis=-1))
        decay = jnp.exp(g_tot + m - m_new)
        wa = jnp.exp(a - m_new[..., None])
        C_new = decay[..., None, None] * C + jnp.einsum('bhs,bhsd,bhsv->bhdv', wa, k_, v_)
        n_new = decay[..., None] * n + jnp.einsum('bhs,bhsd->bhd', wa, k_)
        return (C_new, n_new, m_new), h_out

    init = (jnp.zeros((B, NH, DK, DV), jnp.float32),
            jnp.zeros((B, NH, DK), jnp.float32),
            jnp.zeros((B, NH), jnp.float32))
    _, hs = lax.scan(step, init, (qc, kc, vc, ic, fc))
    hs = hs.transpose(1, 0, 3, 2, 4).reshape(B, S, NH, DV)
    hs = hs * lax.rsqrt(jnp.mean(hs * hs, axis=-1, keepdims=True) + EPS)
    hs = hs * head_gain.astype(jnp.float32).reshape(NH, DV)
    out = hs.reshape(B, S, NH * DV).astype(h.dtype) * jax.nn.sigmoid(o_pre)
    return out @ w_out

def moba_mixer(h, positions, w_qkv, w_out):
    B, S, _ = h.shape
    H, Dh, BLK, QB = ATTN_HEADS, ATTN_DH, MOBA_BLOCK, Q_BLOCK
    q, k, v = jnp.split(h @ w_qkv, 3, axis=-1)
    q = partial_rope(q.reshape(B, S, H, Dh), positions)
    k = partial_rope(k.reshape(B, S, H, Dh), positions)
    v = v.reshape(B, S, H, Dh)
    nb = -(-S // BLK)
    pad = nb * BLK - S
    k = jnp.pad(k, ((0, 0), (0, pad), (0, 0), (0, 0))).astype(jnp.float32)
    v = jnp.pad(v, ((0, 0), (0, pad), (0, 0), (0, 0))).astype(jnp.float32)
    kb = k.transpose(0, 2, 1, 3).reshape(B, H, nb, BLK, Dh)
    vb = v.transpose(0, 2, 1, 3).reshape(B, H, nb, BLK, Dh)
    counts = jnp.minimum(BLK, S - jnp.arange(nb) * BLK).astype(jnp.float32)
    kmean = jnp.sum(kb, axis=3) / counts[:, None]
    topk = min(MOBA_TOPK, nb)
    nqb = S // QB
    qblocks = q.astype(jnp.float32).transpose(0, 2, 1, 3).reshape(B, H, nqb, QB, Dh).transpose(2, 0, 1, 3, 4)
    bi = jnp.arange(B)[:, None, None, None]
    hi = jnp.arange(H)[None, :, None, None]
    scale = Dh ** -0.5
    blk_ids = jnp.arange(nb)

    def attend(args):
        qi, qf = args
        cur = (qi * QB) // BLK
        gate = jnp.einsum('bhqd,bhnd->bhqn', qf, kmean)
        gate = jnp.where(blk_ids < cur, gate, NEG)
        _, idx = lax.top_k(gate, topk)
        sel_ok = idx < cur
        ksel = kb[bi, hi, idx]
        vsel = vb[bi, hi, idx]
        s_sel = jnp.einsum('bhqd,bhqjkd->bhqjk', qf, ksel) * scale
        s_sel = jnp.where(sel_ok[..., None], s_sel, NEG).reshape(B, H, QB, topk * BLK)
        k_own = lax.dynamic_index_in_dim(kb, cur, axis=2, keepdims=False)
        v_own = lax.dynamic_index_in_dim(vb, cur, axis=2, keepdims=False)
        s_own = jnp.einsum('bhqd,bhkd->bhqk', qf, k_own) * scale
        qpos = qi * QB + jnp.arange(QB)
        kpos = cur * BLK + jnp.arange(BLK)
        s_own = jnp.where(kpos[None, :] <= qpos[:, None], s_own, NEG)
        p = jax.nn.softmax(jnp.concatenate([s_sel, s_own], axis=-1), axis=-1)
        p_sel = p[..., :topk * BLK].reshape(B, H, QB, topk, BLK)
        p_own = p[..., topk * BLK:]
        return (jnp.einsum('bhqjk,bhqjkd->bhqd', p_sel, vsel)
                + jnp.einsum('bhqk,bhkd->bhqd', p_own, v_own))

    outs = lax.map(attend, (jnp.arange(nqb), qblocks))
    o = outs.transpose(1, 0, 3, 2, 4).reshape(B, S, H * Dh).astype(h.dtype)
    return o @ w_out

def short_conv_mixer(h, w_in, conv_w, w_out):
    b_gate, c_gate, u = jnp.split(h @ w_in, 3, axis=-1)
    z = c_gate * u
    y = lax.conv_general_dilated(
        z, conv_w[:, None, :].astype(z.dtype), window_strides=(1,), padding=[(CONV_WIDTH - 1, 0)],
        dimension_numbers=('NWC', 'WIO', 'NWC'), feature_group_count=D_MODEL)
    return (b_gate * y) @ w_out

def stick_breaking_mixer(h, w_qkv, w_out):
    B, S, _ = h.shape
    H, Dh, QB = ATTN_HEADS, ATTN_DH, Q_BLOCK
    q, k, v = jnp.split(h @ w_qkv, 3, axis=-1)
    q = q.astype(jnp.float32).reshape(B, S, H, Dh).transpose(0, 2, 1, 3)
    k = k.astype(jnp.float32).reshape(B, S, H, Dh).transpose(0, 2, 1, 3)
    v = v.astype(jnp.float32).reshape(B, S, H, Dh).transpose(0, 2, 1, 3)
    nqb = S // QB
    qblocks = q.reshape(B, H, nqb, QB, Dh).transpose(2, 0, 1, 3, 4)
    kpos = jnp.arange(S)
    scale = Dh ** -0.5

    def attend(args):
        qi, qf = args
        z = jnp.einsum('bhqd,bhkd->bhqk', qf, k) * scale
        qpos = qi * QB + jnp.arange(QB)
        strict = kpos[None, :] < qpos[:, None]
        log_fail = jnp.where(strict, jax.nn.log_sigmoid(-z), 0.0)
        after = lax.cumsum(log_fail, axis=3, reverse=True) - log_fail
        a = jnp.exp(jnp.where(strict, jax.nn.log_sigmoid(z) + after, -jnp.inf))
        return jnp.einsum('bhqk,bhkd->bhqd', a, v)

    outs = lax.map(attend, (jnp.arange(nqb), qblocks))
    o = outs.transpose(1, 0, 3, 2, 4).reshape(B, S, H * Dh).astype(h.dtype)
    return o @ w_out

def swiglu(h, w_gate, w_up, w_down):
    return (jax.nn.silu(h @ w_gate) * (h @ w_up)) @ w_down

def setup_inputs(seed: int = 0) -> dict:
    key = jax.random.key(seed)
    ks = jax.random.split(key, 20)
    D, F = D_MODEL, FFN_HIDDEN
    n_a = (DEPTH + 3) // 4
    n_b = (DEPTH + 2) // 4
    n_c = (DEPTH + 1) // 4
    n_d = DEPTH // 4
    nrm = lambda k, shape, fan: jax.random.normal(k, shape, jnp.float32) * fan ** -0.5
    x = jax.random.normal(ks[0], (BATCH, SEQ, D), jnp.float32)
    positions = jnp.broadcast_to(jnp.arange(SEQ, dtype=jnp.int32), (BATCH, SEQ))
    norm_gains = 1.0 + 0.1 * jax.random.normal(ks[1], (DEPTH, 2, D), jnp.float32)
    mlstm_w_in = nrm(ks[2], (n_a, D, MLSTM_IN), D)
    ib = 0.1 * jax.random.normal(ks[3], (n_a, MLSTM_HEADS), jnp.float32)
    fb = 3.0 + 0.1 * jax.random.normal(ks[4], (n_a, MLSTM_HEADS), jnp.float32)
    mlstm_b_gate = jnp.concatenate([ib, fb], axis=-1)
    mlstm_head_gain = 1.0 + 0.1 * jax.random.normal(ks[5], (n_a, MLSTM_HEADS * MLSTM_DV), jnp.float32)
    mlstm_w_out = nrm(ks[6], (n_a, MLSTM_HEADS * MLSTM_DV, D), MLSTM_HEADS * MLSTM_DV)
    moba_w_qkv = nrm(ks[7], (n_b, D, 3 * D), D)
    moba_w_out = nrm(ks[8], (n_b, D, D), D)
    conv_w_in = nrm(ks[9], (n_c, D, 3 * D), D)
    conv_w = nrm(ks[10], (n_c, CONV_WIDTH, D), CONV_WIDTH)
    conv_w_out = nrm(ks[11], (n_c, D, D), D)
    sb_w_qkv = nrm(ks[12], (n_d, D, 3 * D), D)
    sb_w_out = nrm(ks[13], (n_d, D, D), D)
    ffn_w_gate = nrm(ks[14], (DEPTH, D, F), D)
    ffn_w_up = nrm(ks[15], (DEPTH, D, F), D)
    ffn_w_down = nrm(ks[16], (DEPTH, F, D), F)
    final_gain = 1.0 + 0.1 * jax.random.normal(ks[17], (D,), jnp.float32)
    return {"x": x, "positions": positions, "norm_gains": norm_gains,
            "mlstm_w_in": mlstm_w_in, "mlstm_b_gate": mlstm_b_gate,
            "mlstm_head_gain": mlstm_head_gain, "mlstm_w_out": mlstm_w_out,
            "moba_w_qkv": moba_w_qkv, "moba_w_out": moba_w_out,
            "conv_w_in": conv_w_in, "conv_w": conv_w, "conv_w_out": conv_w_out,
            "sb_w_qkv": sb_w_qkv, "sb_w_out": sb_w_out,
            "ffn_w_gate": ffn_w_gate, "ffn_w_up": ffn_w_up, "ffn_w_down": ffn_w_down,
            "final_gain": final_gain}

def reference(x, positions, norm_gains, mlstm_w_in, mlstm_b_gate, mlstm_head_gain, mlstm_w_out,
              moba_w_qkv, moba_w_out, conv_w_in, conv_w, conv_w_out, sb_w_qkv, sb_w_out,
              ffn_w_gate, ffn_w_up, ffn_w_down, final_gain):
    h = x
    for layer in range(DEPTH):
        kind = layer % N_MIXERS
        j = layer // N_MIXERS
        a = rms_norm(h, norm_gains[layer, 0])
        if kind == 0:
            mix = mlstm_mixer(a, mlstm_w_in[j], mlstm_b_gate[j], mlstm_head_gain[j], mlstm_w_out[j])
        elif kind == 1:
            mix = moba_mixer(a, positions, moba_w_qkv[j], moba_w_out[j])
        elif kind == 2:
            mix = short_conv_mixer(a, conv_w_in[j], conv_w[j], conv_w_out[j])
        else:
            mix = stick_breaking_mixer(a, sb_w_qkv[j], sb_w_out[j])
        h = h + mix
        h = h + swiglu(rms_norm(h, norm_gains[layer, 1]), ffn_w_gate[layer], ffn_w_up[layer], ffn_w_down[layer])
    return rms_norm(h, final_gain)


_drawn_inputs = setup_inputs


def setup_inputs(seed=0):
    import zlib

    import numpy as np

    out = dict(_drawn_inputs(seed))
    spreads = {}
    factors = {}
    for name, (base, spread) in spreads.items():
        noise = np.random.default_rng([zlib.crc32(name.encode()), seed]).standard_normal(out[name].shape)
        drawn = base * np.exp(spread * noise) if base else spread * noise
        out[name] = __import__('jax').numpy.asarray(drawn.astype(out[name].dtype))
    for name, factor in factors.items():
        out[name] = (out[name] * factor).astype(out[name].dtype)
    return out
```

```python
import math

import numpy as np
import concourse.bass as bass
from concourse import mybir
from contextlib import ExitStack

F32, F32R, BF16, I32 = mybir.dt.float32, mybir.dt.float32r, mybir.dt.bfloat16, mybir.dt.int32
ALU = mybir.AluOpType
ACT = mybir.ActivationFunctionType
AX = mybir.AxisListType

P = 128
D = 1024
T = 256
C = D // P
TT = T // P
LAYERS = 4
EPS = 1e-6
MH, MDK, MDV = 4, 128, 256
AH, DH = 16, 64
GROUPS = AH // 4
ROPE_HALF = DH // 8
ROPE_THETA = 500000.0
FFN = 2816
FP = FFN // 256
SLOTS = 3
MIX_PAIRS = 16
LAYER_PAIRS = MIX_PAIRS + 3 * FP
PAIRS = LAYERS * LAYER_PAIRS
NEG = -1e30
TWO_PI = 2 * math.pi
TWO_PI_A = 6.28125
TWO_PI_B = float(np.float32(0.001934051513671875))
TWO_PI_C = TWO_PI - TWO_PI_A - TWO_PI_B
ROUNDER = 12582912.0
PI_F = 3.1415925

ROW_GAIN, ROW_HEAD, ROW_CONV, ROW_ROPE = 0, 64, 72, 96
ROWS = 99
K_PERM, K_SELECT = 0, P
K_COLS = K_SELECT + MH * P
B_IDENT, B_MASK_TS, B_MASK_ST, B_STRICT_ST = range(4)


def shape_constants():
    k = np.zeros((P, K_COLS), np.float32)
    a = np.arange(P)
    inside = a % DH
    partner = np.where(inside < ROPE_HALF, a + ROPE_HALF, np.where(inside < 2 * ROPE_HALF, a - ROPE_HALF, a))
    k[partner, K_PERM + a] = 1.0
    for h in range(MH):
        k[h, K_SELECT + h * P:K_SELECT + (h + 1) * P] = 1.0
    r = np.zeros((3, P), np.float32)
    inv = np.float32(ROPE_THETA) ** (-np.arange(ROPE_HALF, dtype=np.float32) / np.float32(ROPE_HALF))
    rot = inside < 2 * ROPE_HALF
    r[0, rot] = inv[inside[rot] % ROPE_HALF]
    r[1, rot] = np.where(inside[rot] < ROPE_HALF, -1.0, 1.0)
    r[2, rot] = 1.0
    return k, r


def build(nc, x, positions, norm_gains, mlstm_w_in, mlstm_b_gate, mlstm_head_gain, mlstm_w_out,
          moba_w_qkv, moba_w_out, conv_w_in, conv_w, conv_w_out, sb_w_qkv, sb_w_out,
          ffn_w_gate, ffn_w_up, ffn_w_down, final_gain, k_const, rope_rows, out):
    with ExitStack() as ctx:
        def sb(name, shape, dt=F32):
            return ctx.enter_context(nc.sbuf_tensor(name, shape, dt))

        def sem(name):
            return ctx.enter_context(nc.semaphore(name))

        w_raw = sb("w_raw", [P, SLOTS, 2048])
        w_hi = sb("w_hi", [P, SLOTS, 2048], F32R)
        w_lo = sb("w_lo", [P, SLOTS, 2048], F32R)
        resid = sb("resid", [P, C, T])
        act_hi = sb("act_hi", [P, C, T], F32R)
        act_lo = sb("act_lo", [P, C, T], F32R)
        mix_hi = sb("mix_hi", [P, C, T], F32R)
        mix_lo = sb("mix_lo", [P, C, T], F32R)
        sq = sb("sq", [P, 2, 2, T])
        ss = sb("ss", [P, 2, T])
        rms_sd = sb("rms_sd", [P, TT])
        rms_col = sb("rms_col", [P, TT])
        diag = sb("diag", [P, T])
        R_sb = sb("R_sb", [P, T])
        xtok = sb("xtok", [P, TT, D])
        ksb = sb("ksb", [P, K_COLS])
        ident = sb("ident", [P, P])[:, :]
        suffix = sb("suffix", [P, P])[:, :]
        kbf = sb("kbf", [P, 4, P], BF16)
        zeros_bf = sb("zeros_bf", [P, 512], BF16)
        ones = sb("ones", [P, T])
        minus = sb("minus", [P, P])
        eps = sb("eps", [P, 1])
        rows = sb("rows", [ROWS, P])
        cols = sb("cols", [P, ROWS])
        h_hi = sb("h_hi", [P, 2, 2, T], F32R)
        h_lo = sb("h_lo", [P, 2, 2, T], F32R)
        gate_raw = sb("gate_raw", [P, C, 2 * MH])
        gate_hi = mix_hi[:, 0:C // 2, :].rearrange("p a (b n) -> p (a b) n", n=P)
        gate_lo = mix_lo[:, 0:C // 2, :].rearrange("p a (b n) -> p (a b) n", n=P)
        bias_i = sb("bias_i", [MH, 1])
        bias_f = sb("bias_f", [MH, 1])
        gate_sc = sb("gate_sc", [64, T])
        area = sb("phase_area", [P, 9472])
        used = [0]

        def carve(shape, parts=P):
            n = int(np.prod(shape))
            view = area[0:parts, used[0]:used[0] + n]
            used[0] += n
            names = "abcd"[:len(shape)]
            if len(shape) == 1:
                return view
            return view.rearrange("p (" + " ".join(names) + ") -> p " + " ".join(names),
                                  **dict(zip(names, shape)))
        m_q = carve([MH, T])
        m_k = carve([MH, T])
        v_sb = sb("v_sb", [P, TT, D])
        gcol = sb("gcol", [P, 16])
        expnegm = sb("expnegm", [P, 8])
        gr = carve([12, T], MH)
        E = carve([384])
        ST = carve([384])
        nums = carve([MH, 2, T])
        nsq = carve([2, T])
        fc = sb("fc", [P, 8, 8])
        m_diag = carve([MH, T])
        o_sc = xtok[:, :, :].rearrange("p a (b t) -> p (a b) t", t=T)
        mlt = sb("mlt", [P, 2, 2, T])
        mix32 = sb("mix32", [P, 2, 2, T])
        used[0] = 0
        ang = sb("ang", [P, 4, T])
        cos_t = sb("cos_t", [P, T])
        sin_t = sb("sin_t", [P, T])
        cos_r = carve([T])
        sin_r = carve([T])
        q_raw = carve([2, T])
        k_raw = carve([2, T])
        rot1 = carve([2, 2, T])
        rot2 = carve([2, 2, T])
        q_f = carve([2, T])
        k_f = carve([2, T])
        prob = carve([4, 384])
        prob_t = carve([4, 384])
        sp_a = carve([4, 384])
        mx = sb("mx", [P, 8])
        nmx = sb("nmx", [P, 8])
        rsum = sb("rsum", [P, 8])
        rinv = sb("rinv", [P, 8])
        used[0] = 0
        g_sc, u_sc, sil, hid = (carve([2, T]) for _ in range(4))
        final_b = area[:, 4 * 2 * T:4 * 2 * T + D]
        used[0] = 0
        c_sc = carve([2, T])
        cu_sc = carve([2, T])
        b_sc = carve([2, T])
        z_pad = sb("z_pad", [P, 2, T + 2])
        y_sb = carve([2, T])

        ps = ctx.enter_context(nc.psum_tensor("ps", [P, 8, 512], F32))
        LAST_BANKS = (0, 6)
        ACC, NORM, SPARE = 2, 6, 7

        def acc_tile(o):
            return ps[:, ACC + o // 2, (o % 2) * T:(o % 2 + 1) * T]

        def flat(bank, n=2):
            return ps[:, bank, :].rearrange("p (j t) -> p j t", j=n)

        ident_bf = kbf[:, B_IDENT, :]

        def bcast(ap2, n):
            return ap2.unsqueeze(1).to_broadcast([ap2.shape[0], n, ap2.shape[-1]])

        raw_landed = [sem(f"raw_landed{s}") for s in range(SLOTS)]
        x_landed, k_landed, rows_landed = sem("x_landed"), sem("k_landed"), sem("rows_landed")
        gate_landed, bias_landed, pos_landed, fin_landed = (
            sem("gate_landed"), sem("bias_landed"), sem("pos_landed"), sem("fin_landed"))
        out_landed = sem("out_landed")
        hi_ready, lo_ready, pair_used = sem("hi_ready"), sem("lo_ready"), sem("pair_used")
        const_set, kbf_ready = sem("const_set"), sem("kbf_ready")
        cols_ps, cols_ready = sem("cols_ps"), sem("cols_ready")
        acc_done, resid_ready, act_hi_ready, act_lo_ready = (
            sem("acc_done"), sem("resid_ready"), sem("act_hi_ready"), sem("act_lo_ready"))
        sq_ready, ss_squared, ss_added, ident_set = sem("sq_ready"), sem("ss_squared"), sem("ss_added"), sem("ident_set")
        ss_col, sd_ready, diag_ready, rb_ps, R_ready = (
            sem("ss_col"), sem("sd_ready"), sem("diag_ready"), sem("rb_ps"), sem("R_ready"))
        dve_step, act_step, pool_step = sem("dve_step"), sem("act_step"), sem("pool_step")
        g_scaled, u_scaled, silu_done, hid_ready, h_hi_ready, h_lo_ready = (
            sem("g_scaled"), sem("u_scaled"), sem("silu_done"), sem("hid_ready"),
            sem("h_hi_ready"), sem("h_lo_ready"))
        mix_hi_ready, mix_lo_ready = sem("mix_hi_ready"), sem("mix_lo_ready")
        gw_zero, gw_hi, gw_lo, gates_ps = sem("gw_zero"), sem("gw_hi"), sem("gw_lo"), sem("gates_ps")
        f_scaled, f_moved, f_logs, g_rows, gcol_ps, gcol_ready, expm_ready = (
            sem("f_scaled"), sem("f_moved"), sem("f_logs"), sem("g_rows"), sem("gcol_ps"),
            sem("gcol_ready"), sem("expm_ready"))
        m_qk_ready, m_v_ready, m_s1, E_ready, ST_ready, m_s2, num_ready, nsq_ready, m_s3 = (
            sem("m_qk_ready"), sem("m_v_ready"), sem("m_s1"), sem("E_ready"), sem("ST_ready"),
            sem("m_s2"), sem("num_ready"), sem("nsq_ready"), sem("m_s3"))
        m_var, m_sd, m_diag_ready, m_fb, o_scaled, o_sig, m_t_ready, m_mix = (
            sem("m_var"), sem("m_sd"), sem("m_diag_ready"), sem("m_fb"), sem("o_scaled"),
            sem("o_sig"), sem("m_t_ready"), sem("m_mix"))
        trig_ready, ang_ready = sem("trig_ready"), sem("ang_ready")
        qk_raw_ready, perm_done, rot_added, qk_ready, v_ready = (
            sem("qk_raw_ready"), sem("perm_done"), sem("rot_added"), sem("qk_ready"), sem("v_ready"))
        rot_parts = sem("rot_parts")
        scores_done, nmax_ready, exp_done, prob_ready, stage2_done = (
            sem("scores_done"), sem("nmax_ready"), sem("exp_done"),
            sem("prob_ready"), sem("stage2_done"))
        probt_dve, probt_act, pv_done, soft_ready = (
            sem("probt_dve"), sem("probt_act"), sem("pv_done"), sem("soft_ready"))
        conv_evac, z_ready, y_act, y_ready, b_ready, cmix_ready, zpad_set = (
            sem("conv_evac"), sem("z_ready"), sem("y_act"), sem("y_ready"), sem("b_ready"),
            sem("cmix_ready"), sem("zpad_set"))
        fin_ps, fin_ready = sem("fin_ps"), sem("fin_ready")

        def mix_base(layer):
            return layer * LAYER_PAIRS

        def wout_base(layer):
            return mix_base(layer) + 12

        def ffn_base(layer):
            return mix_base(layer) + MIX_PAIRS

        def acc_wait(block, o):
            o |= 1
            if block == 0:
                return acc_done, o + 1
            if o < C - 1:
                return acc_done, C + (C - 1) * (block - 1) + o + 1
            layer = (block - 1) // 2
            last = ffn_base(layer) if block % 2 else ffn_base(layer) + 3 * FP
            return pair_used, last

        gain_col = [[cols[:, ROW_GAIN + b * C + o:ROW_GAIN + b * C + o + 1] for o in range(C)] for b in range(8)]

        def col_view(w):
            return w.rearrange("(k p) n -> p k n", p=P)

        def row_view(w):
            return w.rearrange("(j p) n -> p j n", p=P)

        block_ctx = ctx.enter_context(nc.Block())

        @block_ctx.sync
        def _(sp):
            def load(n, i, src):
                slot, lap = n % SLOTS, n // SLOTS
                if n >= SLOTS:
                    sp.wait_ge(hi_ready, n - 2)
                    sp.wait_ge(lo_ready, n - 2 + 3 * i)
                inner = src.shape[-1]
                dst = w_raw[:, slot, :].rearrange("p (k c) -> p k c", c=inner)
                sp.dma_start(dst, src).then_inc(raw_landed[slot], 16)

            sp.dma_start(xtok[:, 0, :], x[0, 0:P, :]).then_inc(x_landed, 16)
            sp.dma_start(xtok[:, 1, :], x[0, P:T, :]).then_inc(x_landed, 16)
            for layer in range(LAYERS):
                n = mix_base(layer)
                if layer == 0:
                    w = col_view(mlstm_w_in[0])
                    q0, k0, v0, o0 = 0, MH * MDK, 2 * MH * MDK, 2 * MH * MDK + D
                    order = [q0, k0, v0, v0 + 256, q0 + 256, k0 + 256, v0 + 512, v0 + 768,
                             o0, o0 + 256, o0 + 512, o0 + 768]
                    for j, c in enumerate(order):
                        load(n + j, 0, w[:, :, c:c + 256])
                    w_out = mlstm_w_out[0]
                else:
                    w = col_view([None, moba_w_qkv, conv_w_in, sb_w_qkv][layer][0])
                    w_out = [None, moba_w_out, conv_w_out, sb_w_out][layer][0]
                    with sp.Fori(0, GROUPS) as i:
                        for j, c in enumerate((0, D, 2 * D)):
                            load(n + j, i, w[:, :, bass.ds(i * 256 + c, 256)])
                wo = row_view(w_out)
                for j in range(4):
                    load(n + 12 + j, 0, wo[:, 2 * j:2 * j + 2, :])
                g, u, d = col_view(ffn_w_gate[layer]), col_view(ffn_w_up[layer]), row_view(ffn_w_down[layer])
                n = ffn_base(layer)
                load(n, 0, g[:, :, 0:256])
                load(n + 1, 0, u[:, :, 0:256])
                if layer == LAYERS - 1:
                    sp.wait_ge(pair_used, n)
                    sp.dma_start(final_b, final_gain.partition_broadcast(P)).then_inc(fin_landed, 16)
                with sp.Fori(0, FP - 2) as i:
                    load(n + 2, i, g[:, :, bass.ds(i * 256 + 256, 256)])
                    load(n + 3, i, d[:, bass.ds(i * 2, 2), :])
                    load(n + 4, i, u[:, :, bass.ds(i * 256 + 256, 256)])
                last = FP - 1
                load(n + 3 * last - 1, 0, g[:, :, last * 256:])
                load(n + 3 * last, 0, u[:, :, last * 256:])
                load(n + 3 * last + 1, 0, d[:, 2 * last - 2:2 * last, :])
                load(n + 3 * last + 2, 0, d[:, 2 * last:2 * last + 2, :])
            for tt in range(TT):
                sp.wait_ge(fin_ready, 2 * tt + 2)
                sp.dma_start(out[0, tt * P:(tt + 1) * P, :], xtok[:, tt, :]).then_inc(out_landed, 16)
            sp.wait_ge(out_landed, 16 * TT)

        @block_ctx.tensor
        def _(pe):
            def mm(dst, lhsT, rhs, start=False, stop=False):
                return pe.matmul(dst, lhsT, rhs, start=start, stop=stop, skip_group_check=True)

            def split_mm(dst, wh, wl, ah, al, start, stop):
                mm(dst, wh, ah, start=start)
                mm(dst, wh, al)
                return mm(dst, wl, ah, stop=stop)

            def pair_ready(n, i=0):
                pe.wait_ge(hi_ready, n + 1 + 3 * i)
                pe.wait_ge(lo_ready, n + 1 + 3 * i)

            def act_chunk(block, k):
                pe.wait_ge(act_hi_ready, C * block + k + 1)
                pe.wait_ge(act_lo_ready, C * block + k + 1)

            def col_tile(n, j, dst, block=None, clears=False):
                slot = n % SLOTS
                wh = w_hi[:, slot, :].rearrange("p (k c) -> p k c", c=256)
                wl = w_lo[:, slot, :].rearrange("p (k c) -> p k c", c=256)
                for k in range(C):
                    if block is not None:
                        act_chunk(block, k)
                        if k % 2 and clears:
                            mm(ps[:, ACC + k // 2, :], zeros_bf[:, 0:P], zeros_bf[:, :], start=True)
                    last = split_mm(dst, wh[:, k, j * P:(j + 1) * P], wl[:, k, j * P:(j + 1) * P],
                                    act_hi[:, k, :], act_lo[:, k, :], j == 0 and k == 0, k == C - 1)
                return last

            def token_tile(n, tt, dst):
                slot = n % SLOTS
                wh = w_hi[:, slot, :].rearrange("p (k c) -> p k c", c=256)
                wl = w_lo[:, slot, :].rearrange("p (k c) -> p k c", c=256)
                for k in range(C):
                    ah, al = act_hi[:, k, tt * P:(tt + 1) * P], act_lo[:, k, tt * P:(tt + 1) * P]
                    mm(dst, ah, wh[:, k, :], start=(k == 0 and tt == 0))
                    mm(dst, ah, wl[:, k, :])
                    last = mm(dst, al, wh[:, k, :], stop=(k == C - 1))
                return last

            def row_pair(n, ah, al, start=False):
                slot = n % SLOTS
                wh = w_hi[:, slot, :].rearrange("p (j c) -> p j c", j=2)
                wl = w_lo[:, slot, :].rearrange("p (j c) -> p j c", j=2)
                for j in range(2):
                    for o in range(C):
                        last = split_mm(acc_tile(o), wh[:, j, o * P:(o + 1) * P], wl[:, j, o * P:(o + 1) * P],
                                        ah[:, j, :], al[:, j, :], start and j == 0 and o % 2 == 0, False)
                return last

            def last_row_pair(n, ah, al):
                slot = n % SLOTS
                wh = w_hi[:, slot, :].rearrange("p (j c) -> p j c", j=2)
                wl = w_lo[:, slot, :].rearrange("p (j c) -> p j c", j=2)
                for o in range(C):
                    for j in range(2):
                        last = split_mm(acc_tile(o), wh[:, j, o * P:(o + 1) * P], wl[:, j, o * P:(o + 1) * P],
                                        ah[:, j, :], al[:, j, :], False, j == 1)
                    last.then_inc(acc_done if o < C - 1 else pair_used, 1)

            def norm_sums(block):
                pe.wait_ge(ss_added, 3 * (block + 1))
                for tt in range(TT):
                    for half in range(2):
                        last = mm(ps[:, NORM, tt:tt + 1], ss[:, half, tt * P:(tt + 1) * P], ones[:, 0:1],
                                  start=(half == 0), stop=(half == 1))
                last.then_inc(ss_col, 1)

            def norm_broadcast(block):
                pe.wait_ge(diag_ready, block + 1)
                mm(ps[:, NORM, T:2 * T], ones[:, 0:P], diag[:, :], start=True, stop=True).then_inc(rb_ps, 1)

            pe.wait_ge(ident_set, 1)
            pe.wait_ge(const_set, 1)
            pe.wait_ge(rows_landed, 64)
            pe.transpose(ps[:, SPARE, 0:ROWS], rows[:, :], ident[0:ROWS, 0:ROWS]).then_inc(cols_ps, 1)
            pe.wait_ge(x_landed, 32)
            for o in range(C):
                for tt in range(TT):
                    last = pe.transpose(acc_tile(o)[:, tt * P:(tt + 1) * P], xtok[:, tt, o * P:(o + 1) * P], ident)
                last.then_inc(acc_done, 1)

            def mlstm():
                n = mix_base(0)
                pe.wait_ge(gw_hi, 2)
                pe.wait_ge(gw_lo, 2)
                pe.wait_ge(cols_ready, 1)
                for k in range(C):
                    act_chunk(0, k)
                    last = split_mm(ps[:, SPARE, 0:T], gate_hi[:, k, :], gate_lo[:, k, :],
                                    act_hi[:, k, :], act_lo[:, k, :], k == 0, k == C - 1)
                last.then_inc(gates_ps, 1)
                norm_sums(0)
                pair_ready(n)
                col_tile(n, 0, ps[:, 0, 0:T])
                norm_broadcast(0)
                col_tile(n, 1, ps[:, 0, T:2 * T]).then_inc(pair_used, 1)
                pair_ready(n + 1)
                col_tile(n + 1, 0, ps[:, 1, 0:T])
                col_tile(n + 1, 1, ps[:, 1, T:2 * T]).then_inc(pair_used, 1)

                def values(pair, bank):
                    pair_ready(pair)
                    token_tile(pair, 0, ps[:, bank, 0:T])
                    token_tile(pair, 1, ps[:, bank, T:2 * T]).then_inc(pair_used, 1)

                def stage1(h):
                    if h >= 1:
                        pe.wait_ge(ST_ready, h)
                    pe.wait_ge(kbf_ready, 4)
                    pe.wait_ge(k_landed, 16)
                    sel = ksb[0:MH, K_SELECT + h * P:K_SELECT + (h + 1) * P]
                    neg_m = gr[:, 8, :]
                    mm(ps[:, 2, 0:T], sel, neg_m, start=True)
                    mm(ps[:, 2, 0:P], ident_bf, kbf[:, 2, :])
                    mm(ps[:, 2, T:T + P], sel, neg_m[:, P:T])
                    mm(ps[:, 2, T:T + P], ident_bf, kbf[:, 2, :], stop=True)
                    pe.wait_ge(m_qk_ready, 2 * (h // 2) + 2)
                    mm(ps[:, 3, 0:T], m_k[:, h, 0:P], m_q[:, h, :], start=True, stop=True)
                    mm(ps[:, 3, T:T + P], m_k[:, h, P:T], m_q[:, h, P:T], start=True, stop=True).then_inc(m_s1, 1)

                def stage2(h):
                    pe.wait_ge(ST_ready, h + 1)
                    pe.wait_ge(m_v_ready, 2 * h + 2)
                    if h >= 1:
                        pe.wait_ge(num_ready, h)
                    for dv in range(2):
                        c0 = h * MDV + dv * P
                        mm(ps[:, 4, dv * T:(dv + 1) * T], v_sb[:, 0, c0:c0 + P], ST[:, 0:T], start=True)
                        mm(ps[:, 4, dv * T + P:(dv + 1) * T], v_sb[:, 1, c0:c0 + P], ST[:, T:T + P], stop=True)
                    mm(ps[:, 5, 2 * h:2 * h + 1], ST[:, 0:P], ones[:, 0:1], start=True, stop=True)
                    mm(ps[:, 5, 2 * h + 1:2 * h + 2], ST[:, P:T], ones[:, 0:1], start=True)
                    mm(ps[:, 5, 2 * h + 1:2 * h + 2], ST[:, T:T + P], ones[:, 0:1], stop=True).then_inc(m_s2, 1)

                def stage3(h):
                    pe.wait_ge(nsq_ready, h + 1)
                    for tt in range(TT):
                        for dv in range(2):
                            last = mm(ps[:, 5, 8 + 2 * h + tt:9 + 2 * h + tt], nsq[:, dv, tt * P:(tt + 1) * P],
                                      ones[:, 0:1], start=(dv == 0), stop=(dv == 1))
                    last.then_inc(m_s3, 1)

                def queries_keys(pair, bank):
                    pair_ready(pair)
                    col_tile(pair, 0, ps[:, bank, 0:T])
                    col_tile(pair, 1, ps[:, bank, T:2 * T]).then_inc(pair_used, 1)

                pe.wait_ge(f_scaled, 1)
                values(n + 2, SPARE)
                pe.wait_ge(R_ready, 1)
                values(n + 3, NORM)
                pe.wait_ge(g_rows, 1)
                for j, row in enumerate((6, 9)):
                    for tt in range(TT):
                        last = mm(ps[:, 5, 32 + 8 * j + 4 * tt:36 + 8 * j + 4 * tt], gr[:, row, tt * P:(tt + 1) * P],
                                  ident[0:MH, 0:MH], start=True, stop=True)
                last.then_inc(gcol_ps, 1)
                pe.wait_ge(m_qk_ready, 2)
                stage1(0)
                queries_keys(n + 4, 0)
                pe.wait_ge(gcol_ready, 1)
                stage2(0)
                stage1(1)
                queries_keys(n + 5, 1)
                stage3(0)
                stage2(1)
                pe.wait_ge(m_v_ready, 4)
                values(n + 6, SPARE)
                stage3(1)
                stage1(2)
                values(n + 7, NORM)
                stage2(2)
                stage1(3)
                pe.wait_ge(m_qk_ready, 4)
                queries_keys(n + 8, 0)
                stage3(2)
                stage2(3)
                queries_keys(n + 9, 1)
                stage3(3)
                pe.wait_ge(o_scaled, 1)
                queries_keys(n + 10, 0)
                pe.wait_ge(m_diag_ready, 1)
                pe.wait_ge(m_v_ready, 2 * MH)
                for g in range(2):
                    last = mm(ps[:, (SPARE, NORM)[g], :], ones[:, 0:P], m_diag[:, 2 * g:2 * g + 2, :].rearrange("p h t -> p (h t)"),
                              start=True, stop=True)
                last.then_inc(m_fb, 1)
                pe.wait_ge(o_scaled, 2)
                queries_keys(n + 11, 1)

            def attention(layer):
                moba = layer == 1
                n0 = mix_base(layer)
                G0 = 0 if moba else GROUPS
                block = 2 * layer

                def scores(g, banks=(2, 4)):
                    pe.wait_ge(qk_ready, 2 * g + 2 * G0 + 2)
                    for h in range(4):
                        rows_ = slice(DH * (h % 2), DH * (h % 2) + DH)
                        q, k = q_f[rows_, h // 2, :], k_f[rows_, h // 2, :]
                        b = banks[h // 2] + h % 2
                        if moba:
                            mm(ps[:, b, 0:P], q[:, 0:P], k[:, 0:P], start=True)
                            mm(ps[:, b, 0:P], ident_bf, kbf[:, 1, :], stop=True)
                            mm(ps[:, b, P:384], q[:, P:T], k[:, :], start=True)
                            last = mm(ps[:, b, T:384], ident_bf, kbf[:, 1, :], stop=True)
                        else:
                            mm(ps[:, b, 0:T], k[:, 0:P], q[:, :], start=True)
                            mm(ps[:, b, 0:P], ident_bf, kbf[:, 3, :])
                            mm(ps[:, b, T:384], k[:, P:T], q[:, P:T])
                            last = mm(ps[:, b, T:384], ident_bf, kbf[:, 3, :])
                        if h % 2:
                            last.then_inc(scores_done, 1)

                def stage2(g, banks=(2, 4)):
                    for half in range(2):
                        pe.wait_ge(prob_ready, 2 * g + 2 * G0 + half + 1)
                        for h in (2 * half, 2 * half + 1):
                            b = banks[half] + h % 2
                            if moba:
                                pe.transpose(ps[:, b, 0:P], prob[:, h, 0:P], ident)
                                pe.transpose(ps[:, b, P:T], prob[:, h, P:T], ident)
                                last = pe.transpose(ps[:, b, T:384], prob[:, h, T:384], ident)
                            else:
                                mm(ps[:, b, 0:T], suffix, prob[:, h, 0:T])
                                mm(ps[:, b, P:T], minus[:, :], prob[:, h, T:384])
                                last = mm(ps[:, b, T:384], suffix, prob[:, h, T:384], stop=True)
                        last.then_inc(stage2_done, 1)

                def stage3(g, bank=NORM):
                    pe.wait_ge(probt_dve if moba else probt_act, (g + 1) if moba else 2 * g + 2 + GROUPS)
                    if moba:
                        pe.wait_ge(probt_act, g + 1)
                    pe.wait_ge(v_ready, 2 * g + 2 * G0 + 2)
                    pe.wait_ge(mix_hi_ready, 2 * g + C * layer)
                    pe.wait_ge(mix_lo_ready, 2 * g + C * layer)
                    for h in range(4):
                        dst = ps[DH * (h % 2):DH * (h % 2) + DH, bank, (h // 2) * T:(h // 2 + 1) * T]
                        mm(dst, v_sb[:, 0, h * DH:(h + 1) * DH], prob_t[:, h, 0:T], start=True)
                        last = mm(dst[:, P:T], v_sb[:, 1, h * DH:(h + 1) * DH], prob_t[:, h, T:384], stop=True)
                    last.then_inc(pv_done, 1)

                def project(g, part, bank, first=False):
                    n = n0 + part
                    pair_ready(n, g)
                    col_tile(n, 0, ps[:, bank, 0:T], block=block if first and part == 0 else None)
                    if first and part == 1:
                        norm_broadcast(block)
                    col_tile(n, 1, ps[:, bank, T:2 * T]).then_inc(pair_used, 1)
                    if first and part == 0:
                        norm_sums(block)

                def project_v(g):
                    n = n0 + 2
                    pair_ready(n, g)
                    token_tile(n, 0, ps[:, SPARE, 0:T])
                    if moba:
                        for j, raw in enumerate((q_raw, k_raw)):
                            pe.wait_ge(qk_raw_ready, 2 * g + j + 1)
                            mm(ps[:, j, :], ksb[:, K_PERM:K_PERM + P], raw[:, :, :].rearrange("p j t -> p (j t)"),
                               start=True, stop=True).then_inc(perm_done, 1)
                    token_tile(n, 1, ps[:, SPARE, T:2 * T]).then_inc(pair_used, 1)

                project(0, 0, 0, first=True)
                project(0, 1, 1, first=True)
                project_v(0)
                with pe.Fori(0, GROUPS - 1) as g:
                    scores(g)
                    project(g + 1, 0, 0)
                    stage2(g)
                    project(g + 1, 1, 1)
                    stage3(g)
                    project_v(g + 1)
                pe.wait_ge(v_ready, 2 * (G0 + GROUPS))
                pe.wait_ge(mix_hi_ready, C * layer + 2 * GROUPS - 2)
                pe.wait_ge(mix_lo_ready, C * layer + 2 * GROUPS - 2)
                scores(GROUPS - 1, LAST_BANKS)
                wout(layer, 0)
                stage2(GROUPS - 1, LAST_BANKS)
                wout(layer, 1)
                stage3(GROUPS - 1, 0)
                wout(layer, 2)
                wout(layer, 3)

            def conv():
                n0 = mix_base(2)
                def body(c, first):
                    for part, bank in enumerate((SPARE, 0, 1)):
                        if not first:
                            pe.wait_ge(conv_evac, 3 * c + part - 2)
                        pair_ready(n0 + part, c)
                        col_tile(n0 + part, 0, ps[:, bank, 0:T], block=4 if first and part == 0 else None)
                        if first and part == 1:
                            norm_broadcast(4)
                        col_tile(n0 + part, 1, ps[:, bank, T:2 * T]).then_inc(pair_used, 1)
                        if first and part == 0:
                            norm_sums(4)
                body(0, True)
                with pe.Fori(1, GROUPS) as c:
                    body(c, False)

            def wout(layer, p):
                n = wout_base(layer) + p
                pe.wait_ge(mix_hi_ready, C * layer + 2 * p + 2)
                pe.wait_ge(mix_lo_ready, C * layer + 2 * p + 2)
                pair_ready(n)
                ah, al = mix_hi[:, 2 * p:2 * p + 2, :], mix_lo[:, 2 * p:2 * p + 2, :]
                if p < 3:
                    row_pair(n, ah, al, start=(p == 0)).then_inc(pair_used, 1)
                else:
                    last_row_pair(n, ah, al)

            def ffn(layer):
                n = ffn_base(layer)
                block = 2 * layer + 1
                t0 = FP * layer

                def tiles(pair, i, bank, hidden, block=None):
                    pair_ready(pair, i)
                    if hidden is not None:
                        pe.wait_ge((g_scaled, u_scaled)[bank], hidden)
                    col_tile(pair, 0, ps[:, bank, 0:T], block=block, clears=True)
                    if bank == 1 and hidden is None:
                        norm_broadcast(2 * layer + 1)
                    col_tile(pair, 1, ps[:, bank, T:2 * T]).then_inc(pair_used, 1)
                    if block is not None:
                        norm_sums(block)

                def down(pair, i, hidden, set_):
                    pe.wait_ge(h_hi_ready, hidden)
                    pe.wait_ge(h_lo_ready, hidden)
                    pair_ready(pair, i)
                    return row_pair(pair, h_hi[:, set_], h_lo[:, set_])

                tiles(n, 0, 0, None, block=block)
                tiles(n + 1, 0, 1, None)
                with pe.Fori(0, FP - 2) as i:
                    tiles(n + 2, i, 0, i + t0 + 1)
                    down(n + 3, i, i + t0 + 1, 0).then_inc(pair_used, 1)
                    tiles(n + 4, i, 1, i + t0 + 1)
                last = FP - 1
                tiles(n + 3 * last - 1, 0, 0, t0 + last)
                tiles(n + 3 * last, 0, 1, t0 + last)
                down(n + 3 * last + 1, 0, t0 + last, 0).then_inc(pair_used, 1)
                pe.wait_ge(h_hi_ready, t0 + FP)
                pe.wait_ge(h_lo_ready, t0 + FP)
                pair_ready(n + 3 * last + 2)
                last_row_pair(n + 3 * last + 2, h_hi[:, 1], h_lo[:, 1])

            for layer in range(LAYERS):
                if layer == 0:
                    mlstm()
                elif layer == 2:
                    conv()
                else:
                    attention(layer)
                if layer in (0, 2):
                    for p in range(4):
                        wout(layer, p)
                ffn(layer)
            for o in range(C):
                pe.wait_ge(resid_ready, 4 * 8 + max(o // 2, 1) + 1)
                for tt in range(TT):
                    bank = ((0, 1), (SPARE, 2))[tt][o // 4]
                    last = pe.transpose(ps[:, bank, (o % 4) * P:(o % 4 + 1) * P], resid[:, o, tt * P:(tt + 1) * P], ident)
            last.then_inc(fin_ps, 1)
            norm_sums(8)

        @block_ctx.scalar
        def _(act):
            def round_pair(n, i=0):
                if n >= PAIRS:
                    return
                slot, lap = n % SLOTS, n // SLOTS
                act.wait_ge(raw_landed[slot], 16 * (lap + 1) + 16 * i)
                if n >= SLOTS:
                    act.wait_ge(pair_used, n - 2 + 3 * i)
                act.activation(w_hi[:, slot, :], w_raw[:, slot, :], ACT.Copy).then_inc(hi_ready, 1)

            def finish(block):
                act.preload_act_table_set("sqrt_and_others")
                for b in range(C // 2):
                    act.wait_ge(resid_ready, 4 * block + b + 1)
                    for o in (2 * b, 2 * b + 1) if block < 8 else ():
                        act.activation(act_hi[:, o, :], resid[:, o, :], ACT.Copy, scale=gain_col[block][o])\
                           .then_inc(act_hi_ready, 1)
                    if b < 2:
                        act.activation(sq[:, b], resid[:, 2 * b:2 * b + 2, :], ACT.Square).then_inc(sq_ready, 1)

            def norm_root(block):
                act.wait_ge(ss_col, block + 1)
                act.activation(rms_sd[:, :], ps[:, NORM, 0:TT], ACT.Sqrt, bias=eps[:, :], scale=1.0 / D)\
                   .then_inc(sd_ready, 1)

            act.dma_start(rows[ROW_GAIN:ROW_GAIN + 64, :], norm_gains.rearrange("l b (c p) -> (l b c) p", p=P))\
               .then_inc(rows_landed, 16)
            act.dma_start(rows[ROW_HEAD:ROW_HEAD + 8, :], mlstm_head_gain.rearrange("a (c p) -> (a c) p", p=P))\
               .then_inc(rows_landed, 16)
            act.dma_start(rows[ROW_CONV:ROW_CONV + 24, :], conv_w.rearrange("a w (c p) -> (a w c) p", p=P))\
               .then_inc(rows_landed, 16)
            act.dma_start(rows[ROW_ROPE:ROW_ROPE + 3, :], rope_rows).then_inc(rows_landed, 16)
            with nc.allow_non_contiguous_dma(reason="eight gate columns"):
                act.dma_start(gate_raw[:, :, :], col_view(mlstm_w_in[0])[:, :, 3 * D:3 * D + 2 * MH]).then_inc(gate_landed, 16)
                act.dma_start(bias_i[:, :], mlstm_b_gate[0, 0:MH].rearrange("(h a) -> h a", a=1)).then_inc(bias_landed, 16)
                act.dma_start(bias_f[:, :], mlstm_b_gate[0, MH:2 * MH].rearrange("(h a) -> h a", a=1)).then_inc(bias_landed, 16)
            act.dma_start(ksb[:, :], k_const).then_inc(k_landed, 16)
            act.dma_start(ang[:, 1, :].bitcast(I32), positions[0, :].partition_broadcast(P)).then_inc(pos_landed, 16)

            act.wait_ge(gate_landed, 16)
            act.wait_ge(gw_zero, 1)
            act.activation(gate_hi[:, :, 0:MH], gate_raw[:, :, 0:MH], ACT.Copy).then_inc(gw_hi, 1)
            act.activation(gate_hi[:, :, 32:32 + MH], gate_raw[:, :, MH:2 * MH], ACT.Copy).then_inc(gw_hi, 1)
            act.wait_ge(cols_ready, 1)
            act.wait_ge(const_set, 1)
            finish(0)
            norm_root(0)
            for n in range(3):
                round_pair(n)

            def mlstm():
                n = mix_base(0)
                act.preload_act_table_set("natural_log_exp_and_others")
                act.wait_ge(f_scaled, 1)
                act.wait_ge(bias_landed, 32)
                act.activation(gr[:, 1, :], gate_sc[32:32 + MH, :], ACT.Identity, bias=bias_f[:, :]).then_inc(f_moved, 1)
                act.activation(gr[:, 0, :], gate_sc[0:MH, :], ACT.Identity, bias=bias_i[:, :]).then_inc(f_moved, 1)
                act.wait_ge(f_moved, 2)
                act.activation(gr[:, 2, :], gr[:, 1, :], ACT.Abs).then_inc(f_moved, 1)
                act.wait_ge(f_moved, 3)
                act.activation(gr[:, 3, :], gr[:, 2, :], ACT.Exp, scale=-1.0).then_inc(f_moved, 1)
                act.wait_ge(f_moved, 4)
                act.activation(gr[:, 4, :], gr[:, 3, :], ACT.Ln, bias=1.0).then_inc(f_logs, 1)
                round_pair(n + 3)
                round_pair(n + 4)

                def value(h):
                    act.wait_ge(pair_used, n + (3, 4, 7, 8)[h])
                    act.wait_ge(diag_ready, 1)
                    for tt in range(TT):
                        act.activation(v_sb[:, tt, h * MDV:(h + 1) * MDV], flat((SPARE, NORM)[h % 2])[:, tt, :],
                                       ACT.Copy, scale=rms_col[:, tt:tt + 1]).then_inc(m_v_ready, 1)

                def weights(h):
                    act.wait_ge(m_s1, h + 1)
                    act.wait_ge(gcol_ready, 1)
                    for s in range(2):
                        a, b = ((0, T), (T, 384))[s]
                        last = act.activation(E[:, a:b], ps[:, 2, a:b], ACT.Exp, bias=gcol[:, 4 * s + h:4 * s + h + 1])
                    last.then_inc(E_ready, 1)

                value(0)
                round_pair(n + 5)
                value(1)
                round_pair(n + 6)
                act.wait_ge(gcol_ready, 1)
                act.activation(expnegm[:, :], gcol[:, 8:16], ACT.Exp, scale=-1.0).then_inc(expm_ready, 1)
                weights(0)
                round_pair(n + 7)
                weights(1)
                round_pair(n + 8)
                value(2)
                round_pair(n + 9)
                weights(2)
                value(3)
                round_pair(n + 10)
                weights(3)
                round_pair(n + 11)
                round_pair(n + 12)
                act.wait_ge(m_var, 1)
                act.activation(fc[:, 5, :], fc[:, 4, :], ACT.Sqrt, bias=eps[:, :], scale=1.0 / MDV).then_inc(m_sd, 1)

                def out_gate(j):
                    act.wait_ge(o_scaled, j + 1)
                    act.activation(o_sc[:, 2 * j:2 * j + 2, :], o_sc[:, 2 * j:2 * j + 2, :], ACT.Sigmoid).then_inc(o_sig, 1)

                def mixed(h):
                    act.wait_ge(m_mix, h + 1)
                    act.activation(mix_hi[:, 2 * h:2 * h + 2, :], mix32[:, h % 2], ACT.Copy).then_inc(mix_hi_ready, 2)

                for j in range(3):
                    out_gate(j)
                round_pair(n + 13)
                mixed(0)
                mixed(1)
                out_gate(3)
                mixed(2)
                round_pair(n + 14)
                mixed(3)
                mix_tail(0)

            def mix_tail(layer):
                n = wout_base(layer)
                round_pair(n + 3)
                round_pair(n + 4)
                finish(2 * layer + 1)
                round_pair(n + 5)
                round_pair(n + 6)
                norm_root(2 * layer + 1)

            def attention(layer):
                moba = layer == 1
                n0 = mix_base(layer)
                G0 = 0 if moba else GROUPS

                if not moba:
                    act.preload_act_table_set("natural_log_exp_and_others")

                def raw_copy(g, j):
                    if moba:
                        act.wait_ge(pair_used, n0 + j + 1 + 3 * g)
                        act.activation((q_raw, k_raw)[j][:, :, :], flat(j), ACT.Copy).then_inc(qk_raw_ready, 1)

                def value(g, tt):
                    act.wait_ge(pair_used, n0 + 3 + 3 * g)
                    act.activation(v_sb[:, tt, 0:T], flat(SPARE)[:, tt, :], ACT.Copy, scale=rms_col[:, tt:tt + 1])\
                       .then_inc(v_ready, 1)

                def soft1(g, banks=(2, 4)):
                    for half in range(2):
                        hs = slice(2 * half, 2 * half + 2)
                        if moba:
                            act.wait_ge(nmax_ready, 2 * g + half + 1)
                            for h in (2 * half, 2 * half + 1):
                                for tb in range(2):
                                    a, b = ((0, P), (P, 384))[tb]
                                    c = 4 * half + 2 * tb + h % 2
                                    last = act.activation(prob[:, h, a:b], ps[:, banks[half] + h % 2, a:b], ACT.Exp,
                                                          bias=nmx[:, c:c + 1], accum_out=rsum[:, c:c + 1])
                            last.then_inc(exp_done, 1)
                        else:
                            z = ps[:, banks[half]:banks[half] + 2, 0:384]
                            act.wait_ge(scores_done, 2 * g + 2 * G0 + half + 1)
                            act.activation(sp_a[:, hs, :], z, ACT.Abs).then_inc(act_step, 1)
                            act.wait_ge(act_step, 4 * g + 2 * half + 1)
                            act.activation(sp_a[:, hs, :], sp_a[:, hs, :], ACT.Exp, scale=-1.0).then_inc(act_step, 1)
                            act.wait_ge(act_step, 4 * g + 2 * half + 2)
                            act.activation(sp_a[:, hs, :], sp_a[:, hs, :], ACT.Ln, bias=1.0).then_inc(soft_ready, 1)

                def soft2(g, banks=(2, 4)):
                    for half in range(2):
                        hs = slice(2 * half, 2 * half + 2)
                        if moba and half == 0:
                            continue
                        act.wait_ge(stage2_done, 2 * g + 2 * G0 + half + 1)
                        act.activation(prob_t[:, hs, :], ps[:, banks[half]:banks[half] + 2, 0:384],
                                       ACT.Copy if moba else ACT.Exp).then_inc(probt_act, 1)

                def mixed(g, bank=NORM):
                    act.wait_ge(pv_done, g + G0 + 1)
                    act.activation(mix_hi[:, bass.ds(2 * g, 2), :] if not isinstance(g, int) else mix_hi[:, 2 * g:2 * g + 2, :],
                                   flat(bank), ACT.Copy).then_inc(mix_hi_ready, 2)

                raw_copy(0, 0)
                round_pair(n0 + 3)
                act.wait_ge(diag_ready, 2 * layer + 1)
                raw_copy(0, 1)
                round_pair(n0 + 4)
                value(0, 0)
                value(0, 1)
                round_pair(n0 + 5)
                with act.Fori(0, GROUPS - 1) as g:
                    soft1(g)
                    raw_copy(g + 1, 0)
                    round_pair(n0 + 6, g)
                    soft2(g)
                    raw_copy(g + 1, 1)
                    round_pair(n0 + 7, g)
                    mixed(g)
                    value(g + 1, 0)
                    value(g + 1, 1)
                    round_pair(n0 + 8, g)
                soft1(GROUPS - 1, LAST_BANKS)
                soft2(GROUPS - 1, LAST_BANKS)
                mixed(GROUPS - 1, 0)
                mix_tail(layer)

            def conv():
                n0 = mix_base(2)

                def body(c, first):
                    g = c - 1 if not first else 0
                    act.wait_ge(pair_used, n0 + 1 + 3 * c)
                    base = 3 if first else 6
                    round_pair(n0 + base, g)
                    act.wait_ge(pair_used, n0 + 2 + 3 * c)
                    round_pair(n0 + base + 1, g)
                    round_pair(n0 + base + 2, g)
                    act.wait_ge(z_ready, c + 1)
                    for j in range(2):
                        w2 = cols[:, ROW_CONV + 16 + j:ROW_CONV + 17 + j] if first else \
                            cols[:, bass.ds(2 * c + (ROW_CONV + 16 + j), 1)]
                        act.activation(y_sb[:, j, :], z_pad[:, j, 2:T + 2], ACT.Copy, scale=w2).then_inc(y_act, 1)
                    act.wait_ge(cmix_ready, c + 1)
                    dst = mix_hi[:, 0:2, :] if first else mix_hi[:, bass.ds(2 * c, 2), :]
                    act.activation(dst, mix32[:, 0], ACT.Copy).then_inc(mix_hi_ready, 2)
                body(0, True)
                with act.Fori(1, GROUPS) as c:
                    body(c, False)
                mix_tail(2)

            def ffn(layer):
                n = ffn_base(layer)
                t0 = FP * layer
                act.preload_act_table_set("silu_and_others")
                if layer == 0:
                    act.wait_ge(ang_ready, 1)
                    act.activation(ang[:, 2:4, :], ang[:, 2:4, :], ACT.Sin).then_inc(trig_ready, 1)

                def silu(t):
                    act.wait_ge(g_scaled, t + 1)
                    act.activation(sil[:, :, :], g_sc[:, :, :], ACT.Silu).then_inc(silu_done, 1)

                def high(t, set_):
                    act.wait_ge(hid_ready, t + 1)
                    act.activation(h_hi[:, set_], hid[:, :, :], ACT.Copy).then_inc(h_hi_ready, 1)

                round_pair(n + 3)
                silu(t0)
                high(t0, 0)
                round_pair(n + 4)
                with act.Fori(0, FP - 2) as i:
                    silu(i + t0 + 1)
                    round_pair(n + 5, i)
                    round_pair(n + 6, i)
                    high(i + t0 + 1, 0)
                    round_pair(n + 7, i)
                t, m = t0 + FP - 1, n + 3 * FP
                silu(t)
                round_pair(m - 1)
                high(t, 1)
                round_pair(m)
                finish(2 * layer + 2)
                round_pair(m + 1)
                round_pair(m + 2)
                norm_root(2 * layer + 2)

            for layer in range(LAYERS):
                if layer == 0:
                    mlstm()
                elif layer == 2:
                    conv()
                else:
                    attention(layer)
                ffn(layer)

        @block_ctx.vector
        def _(dve):
            steps = [0]

            def link(ins):
                steps[0] += 1
                ins.then_inc(dve_step, 1)
                dve.wait_ge(dve_step, steps[0])

            def low_pair(n, i=0):
                if n >= PAIRS:
                    return
                slot = n % SLOTS
                dve.wait_ge(hi_ready, n + 1 + 3 * i)
                dve.tensor_tensor(w_lo[:, slot, :], w_raw[:, slot, :], w_hi[:, slot, :].bitcast(F32), ALU.subtract)\
                   .then_inc(lo_ready, 1)

            def finish(block):
                def low(o):
                    dve.wait_ge(act_hi_ready, C * block + o + 1)
                    dve.scalar_tensor_tensor(out=act_lo[:, o, :], in0=resid[:, o, :], scalar=gain_col[block][o],
                                             in1=act_hi[:, o, :].bitcast(F32), op0=ALU.mult, op1=ALU.subtract)\
                       .then_inc(act_lo_ready, 1)
                for b in range(C // 2):
                    dve.wait_ge(*acc_wait(block, 2 * b))
                    r = resid[:, 2 * b:2 * b + 2, :]
                    if block == 0:
                        ins = dve.tensor_copy(r, flat(ACC + b))
                    else:
                        ins = dve.tensor_tensor(r, r, flat(ACC + b), ALU.add)
                    ins.then_inc(resid_ready, 1)
                    if b >= 1 and block < 8:
                        low(2 * b - 2)
                        low(2 * b - 1)
                if block < 8:
                    low(C - 2)
                    low(C - 1)

            def norm_diag(block):
                dve.wait_ge(sd_ready, block + 1)
                link(dve.reciprocal(rms_col[:, :], rms_sd[:, :]))
                for tt in range(TT):
                    last = dve.tensor_scalar(diag[:, tt * P:(tt + 1) * P], ident, rms_col[:, tt:tt + 1], None, ALU.mult)
                last.then_inc(diag_ready, 1)

            def norm_row(block):
                dve.wait_ge(rb_ps, block + 1)
                dve.tensor_copy(R_sb[:, :], ps[:, NORM, T:2 * T]).then_inc(R_ready, 1)
                dve.wait_ge(R_ready, block + 1)

            def trig_angles():
                dve.wait_ge(pos_landed, 16)
                inv = cols[:, ROW_ROPE:ROW_ROPE + 1]
                a, n, c, s = (ang[:, j, :] for j in range(4))
                link(dve.tensor_copy(a, ang[:, 1, :].bitcast(I32)))
                link(dve.tensor_scalar(a, a, inv, None, ALU.mult))
                link(dve.tensor_scalar(n, a, 1.0 / TWO_PI, ROUNDER, ALU.mult, ALU.add))
                link(dve.tensor_scalar(n, n, ROUNDER, None, ALU.subtract))
                for part in (TWO_PI_A, TWO_PI_B, TWO_PI_C):
                    link(dve.scalar_tensor_tensor(out=a, in0=n, scalar=-part, in1=a, op0=ALU.mult, op1=ALU.add))
                link(dve.tensor_scalar(s, a, PI_F, -PI_F, ALU.min, ALU.max))
                link(dve.tensor_scalar(n, a, math.pi / 2, -TWO_PI, ALU.is_gt, ALU.mult))
                link(dve.scalar_tensor_tensor(out=c, in0=a, scalar=math.pi / 2, in1=n, op0=ALU.add, op1=ALU.add))
                dve.tensor_scalar(c, c, PI_F, -PI_F, ALU.min, ALU.max).then_inc(ang_ready, 1)

            def trig_tables():
                c, s = ang[:, 2, :], ang[:, 3, :]
                sign, rot = cols[:, ROW_ROPE + 1:ROW_ROPE + 2], cols[:, ROW_ROPE + 2:ROW_ROPE + 3]
                dve.wait_ge(trig_ready, 1)
                link(dve.tensor_scalar(cos_t[:, :], c, -1.0, rot, ALU.add, ALU.mult))
                link(dve.tensor_scalar(cos_t[:, :], cos_t[:, :], 1.0, None, ALU.add))
                link(dve.tensor_scalar(sin_t[:, :], s, sign, None, ALU.mult))

            dve.memset(ones[:, :], 1.0)
            dve.memset(minus[:, :], -1.0)
            dve.memset(eps[:, :], EPS)
            dve.memset(zeros_bf[:, :], 0.0).then_inc(const_set, 1)
            dve.wait_ge(cols_ps, 1)
            dve.tensor_copy(cols[:, :], ps[:, SPARE, 0:ROWS]).then_inc(cols_ready, 1)
            dve.wait_ge(cols_ready, 1)
            for a, w in enumerate((0, 32)):
                dve.wait_ge(gw_hi, a + 1)
                dve.tensor_tensor(gate_lo[:, :, w:w + MH], gate_raw[:, :, a * MH:(a + 1) * MH],
                                  gate_hi[:, :, w:w + MH].bitcast(F32), ALU.subtract).then_inc(gw_lo, 1)
            finish(0)
            norm_diag(0)
            for n in range(3):
                low_pair(n)
            def mlstm():
                n = mix_base(0)
                norm_row(0)
                dve.wait_ge(gates_ps, 1)
                dve.tensor_tensor(gate_sc[0:32 + MH, :], ps[0:32 + MH, SPARE, 0:T], R_sb[0:32 + MH, :], ALU.mult)\
                   .then_inc(f_scaled, 1)

                def scale_qk(j, dst, bank, used):
                    dve.wait_ge(pair_used, used)
                    dve.tensor_tensor(dst, flat(bank), bcast(R_sb[:, :], 2), ALU.mult).then_inc(m_qk_ready, 1)

                scale_qk(0, m_q[:, 0:2, :], 0, n + 1)
                scale_qk(1, m_k[:, 0:2, :], 1, n + 2)
                dve.wait_ge(f_logs, 1)
                link(dve.scalar_tensor_tensor(out=gr[:, 5, :], in0=gr[:, 1, :], scalar=0.0, in1=gr[:, 4, :],
                                              op0=ALU.min, op1=ALU.subtract))
                link(dve.tensor_tensor_scan(gr[:, 7, :], ones[0:MH, :], gr[:, 5, :], 0.0, ALU.mult, ALU.add))
                link(dve.tensor_tensor(gr[:, 6, :], gr[:, 0, :], gr[:, 7, :], ALU.subtract))
                link(dve.tensor_tensor_scan(gr[:, 10, :], gr[:, 6, :], gr[:, 6, :], 0.0, ALU.max, ALU.max))
                link(dve.tensor_tensor(gr[:, 9, :], gr[:, 7, :], gr[:, 10, :], ALU.add))
                dve.tensor_scalar(gr[:, 8, :], gr[:, 10, :], -1.0, None, ALU.mult).then_inc(g_rows, 1)
                low_pair(n + 3)
                dve.wait_ge(gcol_ps, 1)
                dve.tensor_copy(gcol[:, :], ps[:, 5, 32:48]).then_inc(gcol_ready, 1)
                low_pair(n + 4)

                def weigh(h):
                    dve.wait_ge(E_ready, h + 1)
                    dve.scalar_tensor_tensor(out=ST[:, :], in0=ps[:, 3, 0:384], scalar=MDK ** -0.5, in1=E[:, :],
                                             op0=ALU.mult, op1=ALU.mult).then_inc(ST_ready, 1)

                def numer(h):
                    dve.wait_ge(m_s2, h + 1)
                    dve.tensor_copy(nums[:, h], flat(4)).then_inc(num_ready, 1)

                weigh(0)
                low_pair(n + 5)
                trig_angles()
                low_pair(n + 6)
                numer(0)
                weigh(1)
                scale_qk(2, m_q[:, 2:4, :], 0, n + 5)
                low_pair(n + 7)
                numer(1)
                scale_qk(3, m_k[:, 2:4, :], 1, n + 6)
                low_pair(n + 8)
                low_pair(n + 9)
                weigh(2)
                low_pair(n + 10)
                numer(2)
                weigh(3)

                def scale_o(j):
                    dve.wait_ge(pair_used, n + 9 + j)
                    dve.tensor_tensor(o_sc[:, 2 * j:2 * j + 2, :], flat(j % 2), bcast(R_sb[:, :], 2), ALU.mult)\
                       .then_inc(o_scaled, 1)
                scale_o(0)
                low_pair(n + 11)
                numer(3)
                scale_o(1)
                low_pair(n + 12)
                dve.wait_ge(m_s3, MH)
                dve.wait_ge(expm_ready, 1)
                link(dve.tensor_copy(fc[:, 6, :], ps[:, 5, 0:8]))
                link(dve.scalar_tensor_tensor(out=fc[:, 0, :], in0=fc[:, 6, :], scalar=-1.0, in1=fc[:, 6, :],
                                              op0=ALU.mult, op1=ALU.max))
                link(dve.tensor_tensor(fc[:, 1, :].rearrange("p (h t) -> p t h", t=2),
                                       fc[:, 0, :].rearrange("p (h t) -> p t h", t=2),
                                       expnegm[:, :].rearrange("p (t h) -> p t h", t=2), ALU.max))
                link(dve.reciprocal(fc[:, 2, :], fc[:, 1, :]))
                link(dve.tensor_tensor(fc[:, 3, :], fc[:, 2, :], fc[:, 2, :], ALU.mult))
                dve.tensor_tensor(fc[:, 4, :], ps[:, 5, 8:16], fc[:, 3, :], ALU.mult).then_inc(m_var, 1)
                dve.wait_ge(m_sd, 1)
                link(dve.reciprocal(fc[:, 6, :], fc[:, 5, :]))
                link(dve.tensor_tensor(fc[:, 7, :], fc[:, 6, :], fc[:, 2, :], ALU.mult))
                for h in range(MH):
                    for tt in range(TT):
                        last = dve.tensor_scalar(m_diag[:, h, tt * P:(tt + 1) * P], ident,
                                                 fc[:, 7, 2 * h + tt:2 * h + tt + 1], None, ALU.mult)
                last.then_inc(m_diag_ready, 1)
                scale_o(2)
                low_pair(n + 13)
                dve.wait_ge(m_fb, 1)

                def factor(h):
                    if h >= 2:
                        dve.wait_ge(m_mix, h - 1)
                    for dv in range(2):
                        last = dve.scalar_tensor_tensor(
                            out=mlt[:, h % 2, dv, :], in0=nums[:, h, dv, :],
                            scalar=cols[:, ROW_HEAD + 2 * h + dv:ROW_HEAD + 2 * h + dv + 1],
                            in1=ps[:, (SPARE, NORM)[h // 2], (h % 2) * T:(h % 2 + 1) * T], op0=ALU.mult, op1=ALU.mult)
                    last.then_inc(m_t_ready, 1)

                def low(h):
                    dve.wait_ge(mix_hi_ready, 2 * h + 2)
                    dve.tensor_tensor(mix_lo[:, 2 * h:2 * h + 2, :], mix32[:, h % 2],
                                      mix_hi[:, 2 * h:2 * h + 2, :].bitcast(F32), ALU.subtract).then_inc(mix_lo_ready, 2)
                factor(0)
                factor(1)
                low(0)
                low(1)
                factor(2)
                scale_o(3)
                factor(3)
                low(2)
                low_pair(n + 14)
                low(3)
                mix_tail(0)

            def mix_tail(layer):
                n = wout_base(layer)
                low_pair(n + 3)
                low_pair(n + 4)
                finish(2 * layer + 1)
                low_pair(n + 5)
                low_pair(n + 6)
                norm_diag(2 * layer + 1)

            def attention(layer):
                moba = layer == 1
                n0 = mix_base(layer)
                G0 = 0 if moba else GROUPS
                norm_row(2 * layer)
                if moba:
                    link(dve.tensor_tensor(cos_r[:, :], cos_t[:, :], R_sb[:, :], ALU.mult))
                    link(dve.tensor_tensor(sin_r[:, :], sin_t[:, :], R_sb[:, :], ALU.mult))

                def rotate1(g, j):
                    scale = DH ** -0.5 if j == 0 else 1.0
                    if moba:
                        dve.wait_ge(qk_raw_ready, 2 * g + j + 1)
                        dve.scalar_tensor_tensor(out=rot1[:, j], in0=(q_raw, k_raw)[j][:, :, :], scalar=scale,
                                                 in1=bcast(cos_r[:, :], 2), op0=ALU.mult, op1=ALU.mult)
                    else:
                        dve.wait_ge(pair_used, n0 + j + 1 + 3 * g)
                        dve.scalar_tensor_tensor(out=(q_f, k_f)[j][:, :, :], in0=flat(j), scalar=scale,
                                                 in1=bcast(R_sb[:, :], 2), op0=ALU.mult, op1=ALU.mult)\
                           .then_inc(qk_ready, 1)

                def rotate2(g):
                    if moba:
                        for j in range(2):
                            dve.wait_ge(perm_done, 2 * g + j + 1)
                            dve.scalar_tensor_tensor(out=rot2[:, j], in0=flat(j), scalar=DH ** -0.5 if j == 0 else 1.0,
                                                     in1=bcast(sin_r[:, :], 2), op0=ALU.mult, op1=ALU.mult)\
                               .then_inc(rot_parts, 1)
                            dve.wait_ge(rot_parts, 2 * g + j + 1)
                            dve.tensor_tensor((q_f, k_f)[j][:, :, :], rot1[:, j], rot2[:, j], ALU.add)\
                               .then_inc(qk_ready, 1)

                def soft1(g, banks=(2, 4)):
                    for half in range(2):
                        hs = slice(2 * half, 2 * half + 2)
                        if moba:
                            dve.wait_ge(scores_done, 2 * g + half + 1)
                            c, b = 4 * half, banks[half]
                            dve.tensor_reduce(mx[:, c:c + 2], ps[:, b:b + 2, 0:P], AX.X, ALU.max)
                            dve.tensor_reduce(mx[:, c + 2:c + 4], ps[:, b:b + 2, P:384], AX.X, ALU.max)\
                               .then_inc(rot_added, 1)
                            dve.wait_ge(rot_added, 4 * g + half + 1)
                            dve.tensor_scalar(nmx[:, c:c + 4], mx[:, c:c + 4], -1.0, None, ALU.mult).then_inc(nmax_ready, 1)
                        else:
                            dve.wait_ge(soft_ready, 2 * g + half + 1)
                            dve.scalar_tensor_tensor(out=prob[:, hs, :], in0=ps[:, banks[half]:banks[half] + 2, 0:384],
                                                     scalar=0.0, in1=sp_a[:, hs, :], op0=ALU.max, op1=ALU.add)\
                               .then_inc(prob_ready, 1)
                    if moba:
                        for half in range(2):
                            hs = slice(2 * half, 2 * half + 2)
                            c = 4 * half
                            dve.wait_ge(exp_done, 2 * g + half + 1)
                            dve.reciprocal(rinv[:, c:c + 4], rsum[:, c:c + 4]).then_inc(rot_added, 1)
                            dve.wait_ge(rot_added, 4 * g + 3 + half)
                            for (a, b), cc in (((0, P), c), ((P, 384), c + 2)):
                                last = dve.tensor_tensor(prob[:, hs, a:b], prob[:, hs, a:b],
                                                         rinv[:, cc:cc + 2].unsqueeze(2).to_broadcast([P, 2, b - a]), ALU.mult)
                            last.then_inc(prob_ready, 1)

                def soft2(g, banks=(2, 4)):
                    if moba:
                        dve.wait_ge(stage2_done, 2 * g + 1)
                        dve.tensor_copy(prob_t[:, 0:2, :], ps[:, banks[0]:banks[0] + 2, 0:384]).then_inc(probt_dve, 1)

                def mixed(g, bank=NORM):
                    dve.wait_ge(mix_hi_ready, 2 * g + C * layer + 2)
                    a, b = ((m[:, bass.ds(2 * g, 2), :] if not isinstance(g, int) else m[:, 2 * g:2 * g + 2, :])
                            for m in (mix_lo, mix_hi))
                    dve.tensor_tensor(a, flat(bank), b.bitcast(F32), ALU.subtract).then_inc(mix_lo_ready, 2)

                rotate1(0, 0)
                low_pair(n0 + 3)
                rotate1(0, 1)
                low_pair(n0 + 4)
                rotate2(0)
                low_pair(n0 + 5)
                with dve.Fori(0, GROUPS - 1) as g:
                    soft1(g)
                    rotate1(g + 1, 0)
                    low_pair(n0 + 6, g)
                    soft2(g)
                    rotate1(g + 1, 1)
                    low_pair(n0 + 7, g)
                    mixed(g)
                    rotate2(g + 1)
                    low_pair(n0 + 8, g)
                soft1(GROUPS - 1, LAST_BANKS)
                soft2(GROUPS - 1, LAST_BANKS)
                mixed(GROUPS - 1, 0)
                mix_tail(layer)

            def conv():
                n0 = mix_base(2)
                norm_row(4)

                def body(c, first):
                    g = c - 1 if not first else 0
                    base = 3 if first else 6

                    def evac(part, dst, bank):
                        dve.wait_ge(pair_used, n0 + part + 1 + 3 * c)
                        dve.tensor_tensor(dst[:, :, :], flat(bank), bcast(R_sb[:, :], 2), ALU.mult).then_inc(conv_evac, 1)
                        low_pair(n0 + base + part, g)
                    evac(0, b_sc, SPARE)
                    evac(1, c_sc, 0)
                    evac(2, cu_sc, 1)
                    for tap in (1, 0):
                        for j in range(2):
                            if tap == 1:
                                dve.wait_ge(y_act, 2 * c + j + 1)
                            else:
                                dve.wait_ge(y_ready, 4 * c + j + 1)
                            col = ROW_CONV + 8 * tap + j
                            w = cols[:, col:col + 1] if first else cols[:, bass.ds(2 * c + col, 1)]
                            dve.scalar_tensor_tensor(out=y_sb[:, j, :], in0=z_pad[:, j, tap:tap + T], scalar=w,
                                                     in1=y_sb[:, j, :], op0=ALU.mult, op1=ALU.add).then_inc(y_ready, 1)
                    dve.wait_ge(mix_hi_ready, C * 2 + 2 * c + 2)
                    lo, hi = ((m[:, 0:2, :] if first else m[:, bass.ds(2 * c, 2), :]) for m in (mix_lo, mix_hi))
                    dve.tensor_tensor(lo, mix32[:, 0], hi.bitcast(F32), ALU.subtract).then_inc(mix_lo_ready, 2)
                body(0, True)
                with dve.Fori(1, GROUPS) as c:
                    body(c, False)
                mix_tail(2)

            def ffn(layer):
                n = ffn_base(layer)
                t0 = FP * layer
                norm_row(2 * layer + 1)

                def scale(dst, signal, pair, bank):
                    dve.wait_ge(pair_used, pair + 1)
                    dve.tensor_tensor(dst[:, :, :], flat(bank), bcast(R_sb[:, :], 2), ALU.mult).then_inc(signal, 1)

                def ups(pair, t, set_):
                    scale(u_sc, u_scaled, pair, 1)
                    dve.wait_ge(silu_done, t + 1)
                    dve.wait_ge(u_scaled, t + 1)
                    dve.tensor_tensor(hid[:, :, :], sil[:, :, :], u_sc[:, :, :], ALU.mult).then_inc(hid_ready, 1)
                    dve.wait_ge(h_hi_ready, t + 1)
                    dve.tensor_tensor(h_lo[:, set_], hid[:, :, :], h_hi[:, set_].bitcast(F32), ALU.subtract)\
                       .then_inc(h_lo_ready, 1)

                scale(g_sc, g_scaled, n, 0)
                low_pair(n + 3)
                ups(n + 1, t0, 0)
                low_pair(n + 4)
                if layer == 0:
                    trig_tables()
                with dve.Fori(0, FP - 2) as i:
                    scale(g_sc, g_scaled, 3 * i + (n + 2), 0)
                    low_pair(n + 5, i)
                    low_pair(n + 6, i)
                    ups(3 * i + (n + 4), i + t0 + 1, 0)
                    low_pair(n + 7, i)
                t, m = t0 + FP - 1, n + 3 * FP
                scale(g_sc, g_scaled, m - 4, 0)
                low_pair(m - 1)
                ups(m - 3, t, 1)
                low_pair(m)
                finish(2 * layer + 2)
                low_pair(m + 1)
                low_pair(m + 2)
                if layer < LAYERS - 1:
                    norm_diag(2 * layer + 2)

            for layer in range(LAYERS):
                if layer == 0:
                    mlstm()
                elif layer == 2:
                    conv()
                else:
                    attention(layer)
                ffn(layer)
            dve.wait_ge(sd_ready, 9)
            link(dve.reciprocal(rms_col[:, :], rms_sd[:, :]))
            dve.wait_ge(fin_ps, 1)
            dve.wait_ge(fin_landed, 16)
            for tt in range(TT):
                for half in range(2):
                    bank = ((0, 1), (SPARE, 2))[tt][half]
                    dve.scalar_tensor_tensor(out=xtok[:, tt, half * 512:(half + 1) * 512], in0=ps[:, bank, :],
                                             scalar=rms_col[:, tt:tt + 1], in1=final_b[:, half * 512:(half + 1) * 512],
                                             op0=ALU.mult, op1=ALU.mult).then_inc(fin_ready, 1)

        @block_ctx.gpsimd
        def _(pool):
            pool.memset(ident, 0.0).then_inc(pool_step, 1)
            pool.wait_ge(pool_step, 1)
            pool.affine_select(out=ident, in_=ident, compare_op=ALU.not_equal, fill=1.0, base=0,
                               pattern=[[-1, P]], channel_multiplier=1).then_inc(ident_set, 1)
            pool.memset(gate_hi[:, :, :].bitcast(F32), 0.0)
            pool.memset(gate_lo[:, :, :].bitcast(F32), 0.0).then_inc(gw_zero, 1)
            pool.memset(z_pad[:, :, 0:2], 0.0)
            pool.memset(kbf[:, :, :], 0.0)
            pool.memset(suffix, 0.0).then_inc(pool_step, 1)
            pool.wait_ge(pool_step, 2)
            for dst, compare, fill, base, sign in (
                    (kbf[:, B_IDENT, :], ALU.not_equal, 1.0, 0, 1),
                    (kbf[:, B_MASK_TS, :], ALU.is_ge, NEG, 0, 1),
                    (kbf[:, B_MASK_ST, :], ALU.is_ge, NEG, 0, -1),
                    (kbf[:, B_STRICT_ST, :], ALU.is_gt, NEG, 0, -1),
                    (suffix, ALU.is_gt, -1.0, 0, -1)):
                pool.affine_select(out=dst, in_=dst, compare_op=compare, fill=fill, base=base,
                                   pattern=[[-sign, P]], channel_multiplier=sign).then_inc(kbf_ready, 1)

            def sum_squares(block):
                n, r = 3 * block, 4 * block
                pool.wait_ge(sq_ready, 2 * block + 2)
                pool.tensor_tensor(ss[:, :, :], sq[:, 0], sq[:, 1], ALU.add).then_inc(ss_added, 1)
                pool.wait_ge(ss_added, n + 1)
                for b in (2, 3):
                    pool.wait_ge(resid_ready, r + b + 1)
                    rr = resid[:, 2 * b:2 * b + 2, :]
                    pool.tensor_tensor(sq[:, b - 2], rr, rr, ALU.mult).then_inc(ss_squared, 1)
                    pool.wait_ge(ss_squared, 2 * block + b - 1)
                    if b == 3:
                        pool.wait_ge(ss_added, n + 2)
                    pool.tensor_tensor(ss[:, :, :], ss[:, :, :], sq[:, b - 2], ALU.add).then_inc(ss_added, 1)

            sum_squares(0)
            for h in range(MH):
                pool.wait_ge(num_ready, h + 1)
                if h >= 1:
                    pool.wait_ge(m_s3, h)
                pool.tensor_tensor(nsq[:, :, :], nums[:, h], nums[:, h], ALU.mult).then_inc(nsq_ready, 1)
            for h in range(MH):
                pool.wait_ge(m_t_ready, h + 1)
                pool.wait_ge(o_sig, h + 1)
                if h >= 2:
                    pool.wait_ge(mix_lo_ready, 2 * h - 2)
                pool.tensor_tensor(mix32[:, h % 2], mlt[:, h % 2], o_sc[:, 2 * h:2 * h + 2, :], ALU.mult).then_inc(m_mix, 1)
            sum_squares(1)
            sum_squares(2)
            sum_squares(3)
            sum_squares(4)
            with pool.Fori(0, GROUPS) as c:
                pool.wait_ge(conv_evac, 3 * c + 3)
                pool.tensor_tensor(z_pad[:, :, 2:T + 2], c_sc[:, :, :], cu_sc[:, :, :], ALU.mult).then_inc(z_ready, 1)
                pool.wait_ge(y_ready, 4 * c + 4)
                pool.tensor_tensor(mix32[:, 0], y_sb[:, :, :], b_sc[:, :, :], ALU.mult).then_inc(cmix_ready, 1)
            for block in range(5, 9):
                sum_squares(block)


_INS = ["x", "positions", "norm_gains", "mlstm_w_in", "mlstm_b_gate", "mlstm_head_gain", "mlstm_w_out",
        "moba_w_qkv", "moba_w_out", "conv_w_in", "conv_w", "conv_w_out", "sb_w_qkv", "sb_w_out",
        "ffn_w_gate", "ffn_w_up", "ffn_w_down", "final_gain"]


def kernel(**inputs):
    import numpy as _np
    import concourse.bacc as _bacc
    from concourse import mybir as _mybir
    from concourse.bass_utils import run_bass_kernel_spmd as _run

    nc = _bacc.Bacc("TRN2", target_bir_lowering=False, num_devices=1)
    arrays, args = {}, []
    constants, rope_rows = shape_constants()
    given = {name: _np.ascontiguousarray(inputs[name]) for name in _INS}
    given["k_const"], given["rope_rows"] = constants, rope_rows
    for name, a in given.items():
        arrays[f"in_{name}"] = a
        args.append(nc.dram_tensor(f"in_{name}", a.shape, _mybir.dt.from_np(a.dtype), kind="ExternalInput").ap())
    args.append(nc.dram_tensor("out_0", (1, T, D), _mybir.dt.float32, kind="ExternalOutput").ap())
    build(nc, *args)
    r = _run(nc, [arrays], core_ids=[0])
    return r.results[0]["out_0"]
```

```python
import math

import numpy as np
import concourse.bass as bass
from concourse import mybir
from contextlib import ExitStack

F32, F32R, BF16, I32 = mybir.dt.float32, mybir.dt.float32r, mybir.dt.bfloat16, mybir.dt.int32
ALU = mybir.AluOpType
ACT = mybir.ActivationFunctionType
AX = mybir.AxisListType

P = 128
D = 1024
T = 256
C = D // P
TT = T // P
LAYERS = 4
EPS = 1e-6
MH, MDK, MDV = 4, 128, 256
AH, DH = 16, 64
GROUPS = AH // 4
ROPE_HALF = DH // 8
ROPE_THETA = 500000.0
FFN = 2816
FP = FFN // 256
SLOTS = 3
MIX_PAIRS = 16
LAYER_PAIRS = MIX_PAIRS + 3 * FP
PAIRS = LAYERS * LAYER_PAIRS
NEG = -1e30
TWO_PI = 2 * math.pi
TWO_PI_A = 6.28125
TWO_PI_B = float(np.float32(0.001934051513671875))
TWO_PI_C = TWO_PI - TWO_PI_A - TWO_PI_B
ROUNDER = 12582912.0
PI_F = 3.1415925

ROW_GAIN, ROW_HEAD, ROW_CONV, ROW_ROPE = 0, 64, 72, 96
ROWS = 99
G_I, G_F, G_LN, G_LS, G_B, G_C, G_MAX, G_M = range(8)
G_NEG = G_F
B_IDENT, B_MASK_TS, B_MASK_ST, B_STRICT_ST = range(4)


def shape_constants():
    k = np.zeros((P, P), np.float32)
    a = np.arange(P)
    inside = a % DH
    partner = np.where(inside < ROPE_HALF, a + ROPE_HALF, np.where(inside < 2 * ROPE_HALF, a - ROPE_HALF, a))
    k[partner, a] = 1.0
    r = np.zeros((3, P), np.float32)
    inv = np.float32(ROPE_THETA) ** (-np.arange(ROPE_HALF, dtype=np.float32) / np.float32(ROPE_HALF))
    rot = inside < 2 * ROPE_HALF
    r[0, rot] = inv[inside[rot] % ROPE_HALF]
    r[1, rot] = np.where(inside[rot] < ROPE_HALF, -1.0, 1.0)
    r[2, rot] = 1.0
    return k, r


def build(nc, x, positions, norm_gains, mlstm_w_in, mlstm_b_gate, mlstm_head_gain, mlstm_w_out,
          moba_w_qkv, moba_w_out, conv_w_in, conv_w, conv_w_out, sb_w_qkv, sb_w_out,
          ffn_w_gate, ffn_w_up, ffn_w_down, final_gain, perm_const, rope_rows, out):
    with ExitStack() as ctx:
        def sb(name, shape, dt=F32):
            return ctx.enter_context(nc.sbuf_tensor(name, shape, dt))

        def sem(name):
            return ctx.enter_context(nc.semaphore(name))

        w_raw = sb("w_raw", [P, SLOTS, 2048])
        w_hi = sb("w_hi", [P, SLOTS, 2048], F32R)
        w_lo = sb("w_lo", [P, SLOTS, 2048], F32R)
        resid = sb("resid", [P, C, T])
        act_hi = sb("act_hi", [P, C, T], F32R)
        act_lo = sb("act_lo", [P, C, T], F32R)
        mix_hi = sb("mix_hi", [P, C, T], F32R)
        mix_lo = sb("mix_lo", [P, C, T], F32R)
        sq = sb("sq", [P, 2, 2, T])
        ss = sb("ss", [P, 2, T])
        rms_sd = sb("rms_sd", [P, TT])
        rms_col = sb("rms_col", [P, TT])
        diag = sb("diag", [P, T])
        R_sb = sb("R_sb", [P, T])
        xtok = sb("xtok", [P, TT, D])
        select = sb("select", [MH, MH * P])
        perm = sb("perm", [P, P], F32R)
        ident = sb("ident", [P, P])[:, :]
        suffix = sb("suffix", [P, P], F32R)
        kbf = sb("kbf", [P, 4, P], BF16)
        zeros_bf = sb("zeros_bf", [P, 512], BF16)
        ones = sb("ones", [P, T])
        minus = sb("minus", [P, P], F32R)
        eps = sb("eps", [P, 1])
        rows = sb("rows", [ROWS, P])
        cols = sb("cols", [P, ROWS])
        part_hi = sb("part_hi", [P, 1536], F32R)
        part_lo = sb("part_lo", [P, 1536], F32R)
        h_hi, h_lo, qk_hi, qk_lo = (
            part[:, 0:4 * T].rearrange("p (a j t) -> p a j t", a=2, j=2) for part in (part_hi, part_lo) * 2)
        soft_hi, soft_lo = (part[:, :].rearrange("p (h s) -> p h s", h=4) for part in (part_hi, part_lo))
        fin_sums = sb("fin_sums", [P, 2, TT])
        gate_raw = sb("gate_raw", [P, C, 2 * MH])
        gate_hi = mix_hi[:, 0:C // 2, :].rearrange("p a (b n) -> p (a b) n", n=P)
        gate_lo = mix_lo[:, 0:C // 2, :].rearrange("p a (b n) -> p (a b) n", n=P)
        bias_i = sb("bias_i", [MH, 1])
        bias_f = sb("bias_f", [MH, 1])
        gate_sc = sb("gate_sc", [64, T])
        area = sb("phase_area", [P, 8448])
        used = [0]

        def carve(shape, parts=P):
            n = int(np.prod(shape))
            view = area[0:parts, used[0]:used[0] + n]
            used[0] += n
            names = "abcd"[:len(shape)]
            if len(shape) == 1:
                return view
            return view.rearrange("p (" + " ".join(names) + ") -> p " + " ".join(names),
                                  **dict(zip(names, shape)))
        m_q = carve([MH, T])
        m_k = carve([MH, T])
        v_sb = sb("v_sb", [P, TT, D])
        gcol = sb("gcol", [P, 16])
        expnegm = sb("expnegm", [P, 8])
        gr = carve([8, T], MH)
        E = carve([384])
        ST = carve([384])
        nums = carve([MH, 2, T])
        nsq = carve([2, T])
        fc = sb("fc", [P, 8, 8])
        m_diag = carve([MH, T])
        perm_raw, suffix_raw = (m_diag[:, 0, a * P:(a + 1) * P] for a in range(2))
        o_sc = xtok[:, :, :].rearrange("p a (b t) -> p (a b) t", t=T)
        mlt = sb("mlt", [P, 2, 2, T])
        mix32 = sb("mix32", [P, 2, 2, T])
        used[0] = 0
        ang = sb("ang", [P, 4, T])
        cos_t = sb("cos_t", [P, T])
        sin_t = sb("sin_t", [P, T])
        cos_r = carve([T])
        sin_r = carve([T])
        rot1 = carve([2, 2, T])
        rot2 = carve([2, 2, T])
        q_f = carve([2, T])
        k_f = carve([2, T])
        prob = carve([4, 384])
        prob_t = carve([4, 384])
        sp_a = carve([4, 384])
        mx = sb("mx", [P, 8])
        nmx = sb("nmx", [P, 8])
        rsum = sb("rsum", [P, 8])
        rinv = sb("rinv", [P, 8])
        used[0] = 0
        g_sc, u_sc, sil, hid = (carve([2, T]) for _ in range(4))
        final_b = area[:, 4 * 2 * T:4 * 2 * T + D]
        used[0] = 0
        c_sc = carve([2, T])
        cu_sc = carve([2, T])
        b_sc = carve([2, T])
        z_pad = sb("z_pad", [P, 2, T + 2])
        y_sb = carve([2, T])

        ps = ctx.enter_context(nc.psum_tensor("ps", [P, 8, 512], F32))
        LAST_BANKS = (0, 6)
        FINAL_BANKS = ((0, 1), (7, 2))
        ACC, NORM, SPARE = 2, 6, 7

        def acc_tile(o):
            return ps[:, ACC + o // 2, (o % 2) * T:(o % 2 + 1) * T]

        def flat(bank, n=2):
            return ps[:, bank, :].rearrange("p (j t) -> p j t", j=n)

        ident_bf = kbf[:, B_IDENT, :]

        def bcast(ap2, n):
            return ap2.unsqueeze(1).to_broadcast([ap2.shape[0], n, ap2.shape[-1]])

        half_landed, half_hi, half_lo = sem("half_landed"), sem("half_hi"), sem("half_lo")
        raw_landed = [sem(f"raw_landed{s}") for s in range(SLOTS)]
        x_landed, k_landed, rows_landed = sem("x_landed"), sem("k_landed"), sem("rows_landed")
        gate_landed, bias_landed, pos_landed, fin_landed = (
            sem("gate_landed"), sem("bias_landed"), sem("pos_landed"), sem("fin_landed"))
        out_landed = sem("out_landed")
        hi_ready, lo_ready, pair_used = sem("hi_ready"), sem("lo_ready"), sem("pair_used")
        const_set, kbf_ready = sem("const_set"), sem("kbf_ready")
        cols_ps, cols_ready = sem("cols_ps"), sem("cols_ready")
        acc_done, resid_ready, act_hi_ready, act_lo_ready = (
            sem("acc_done"), sem("resid_ready"), sem("act_hi_ready"), sem("act_lo_ready"))
        sq_ready, ss_added, ident_set = sem("sq_ready"), sem("ss_added"), sem("ident_set")
        own_squared = sem("own_squared")
        last_squared, ss_complete = sem("last_squared"), sem("ss_complete")
        ss_col, sd_ready, diag_ready, rb_ps, R_ready = (
            sem("ss_col"), sem("sd_ready"), sem("diag_ready"), sem("rb_ps"), sem("R_ready"))
        dve_step, softplus_step, pool_cleared = sem("dve_step"), sem("softplus_step"), sem("pool_cleared")
        g_scaled, u_scaled, silu_done, hid_ready, h_hi_ready, h_lo_ready = (
            sem("g_scaled"), sem("u_scaled"), sem("silu_done"), sem("hid_ready"),
            sem("h_hi_ready"), sem("h_lo_ready"))
        mix_hi_ready, mix_lo_ready = sem("mix_hi_ready"), sem("mix_lo_ready")
        gw_zero, gw_hi, gw_lo, gates_ps = sem("gw_zero"), sem("gw_hi"), sem("gw_lo"), sem("gates_ps")
        f_scaled, f_moved, f_logs, g_rows, gcol_ps, gcol_ready, expm_ready = (
            sem("f_scaled"), sem("f_moved"), sem("f_logs"), sem("g_rows"), sem("gcol_ps"),
            sem("gcol_ready"), sem("expm_ready"))
        m_qk_ready, m_v_ready, m_s1, E_ready, ST_ready, m_s2, num_ready, nsq_ready, m_s3 = (
            sem("m_qk_ready"), sem("m_v_ready"), sem("m_s1"), sem("E_ready"), sem("ST_ready"),
            sem("m_s2"), sem("num_ready"), sem("nsq_ready"), sem("m_s3"))
        m_var, m_sd, m_diag_ready, m_fb, o_scaled, o_sig, m_t_ready, m_mix = (
            sem("m_var"), sem("m_sd"), sem("m_diag_ready"), sem("m_fb"), sem("o_scaled"),
            sem("o_sig"), sem("m_t_ready"), sem("m_mix"))
        trig_ready, ang_ready = sem("trig_ready"), sem("ang_ready")
        qk_raw_ready, perm_done, softmax_step, qk_ready, v_ready = (
            sem("qk_raw_ready"), sem("perm_done"), sem("softmax_step"), sem("qk_ready"), sem("v_ready"))
        rot_turned = sem("rot_turned")
        scores_done, nmax_ready, exp_done, prob_ready, stage2_done = (
            sem("scores_done"), sem("nmax_ready"), sem("exp_done"),
            sem("prob_ready"), sem("stage2_done"))
        probt_dve, probt_act, pv_done, soft_ready = (
            sem("probt_dve"), sem("probt_act"), sem("pv_done"), sem("soft_ready"))
        log_ready, soft_hi_ready, qk_lo_ready = sem("log_ready"), sem("soft_hi_ready"), sem("qk_lo_ready")
        conv_evac, z_ready, y_act, y_ready, cmix_ready = (
            sem("conv_evac"), sem("z_ready"), sem("y_act"), sem("y_ready"), sem("cmix_ready"))
        fin_gained, exact_ready, select_ready = sem("fin_gained"), sem("exact_ready"), sem("select_ready")
        fin_ps, fin_squared, fin_summed, fin_rms = sem("fin_ps"), sem("fin_squared"), sem("fin_summed"), sem("fin_rms")
        fin_ready = [sem(f"fin_ready{tt}") for tt in range(TT)]

        def mix_base(layer):
            return layer * LAYER_PAIRS

        def wout_base(layer):
            return mix_base(layer) + 12

        def ffn_base(layer):
            return mix_base(layer) + MIX_PAIRS

        def second_of(block):
            return (ffn_base(block // 2) if block % 2 else mix_base(block // 2)) + 1

        def acc_wait(block, o):
            o |= 1
            if block == 0:
                return acc_done, o + 1
            if o < C - 1:
                return acc_done, C + (C - 1) * (block - 1) + o + 1
            layer = (block - 1) // 2
            last = ffn_base(layer) if block % 2 else ffn_base(layer) + 3 * FP
            return pair_used, last

        gain_col = [[cols[:, ROW_GAIN + b * C + o:ROW_GAIN + b * C + o + 1] for o in range(C)] for b in range(8)]

        def col_view(w):
            return w.rearrange("(k p) n -> p k n", p=P)

        def row_view(w):
            return w.rearrange("(j p) n -> p j n", p=P)

        block_ctx = ctx.enter_context(nc.Block())

        @block_ctx.sync
        def _(sp):
            def load(n, i, src):
                slot = n % SLOTS
                if n >= SLOTS:
                    sp.wait_ge(hi_ready, n - 2)
                    sp.wait_ge(lo_ready, n - 2 + 3 * i)
                inner = src.shape[-1]
                dst = w_raw[:, slot, :].rearrange("p (k c) -> p k c", c=inner)
                if n == 0:
                    sp.dma_start(dst[:, 0:C // 2], src[:, 0:C // 2]).then_inc(half_landed, 16)
                    dst, src = dst[:, C // 2:], src[:, C // 2:]
                sp.dma_start(dst, src).then_inc(raw_landed[slot], 16)

            sp.dma_start(xtok[:, 0, :], x[0, 0:P, :]).then_inc(x_landed, 16)
            sp.dma_start(xtok[:, 1, :], x[0, P:T, :]).then_inc(x_landed, 16)
            sp.dma_start(rows[ROW_CONV:ROW_CONV + 24, :], conv_w.rearrange("a w (c p) -> (a w c) p", p=P))\
              .then_inc(rows_landed, 16)
            sp.dma_start(rows[ROW_ROPE:ROW_ROPE + 3, :], rope_rows).then_inc(rows_landed, 16)
            for layer in range(LAYERS):
                n = mix_base(layer)
                if layer == 0:
                    w = col_view(mlstm_w_in[0])
                    q0, k0, v0, o0 = 0, MH * MDK, 2 * MH * MDK, 2 * MH * MDK + D
                    order = [q0, k0, v0, v0 + 256, q0 + 256, k0 + 256, v0 + 512, v0 + 768,
                             o0, o0 + 256, o0 + 512, o0 + 768]
                    for j, c in enumerate(order):
                        if j == SLOTS:
                            sp.dma_start(perm_raw, perm_const).then_inc(k_landed, 16)
                            sp.dma_start(ang[:, 1, :].bitcast(I32), positions[0, :].partition_broadcast(P))\
                              .then_inc(pos_landed, 16)
                        load(n + j, 0, w[:, :, c:c + 256])
                    w_out = mlstm_w_out[0]
                else:
                    w = col_view([None, moba_w_qkv, conv_w_in, sb_w_qkv][layer][0])
                    w_out = [None, moba_w_out, conv_w_out, sb_w_out][layer][0]
                    with sp.Fori(0, GROUPS) as i:
                        for j, c in enumerate((0, D, 2 * D)):
                            load(n + j, i, w[:, :, bass.ds(i * 256 + c, 256)])
                wo = row_view(w_out)
                for j in range(4):
                    load(n + 12 + j, 0, wo[:, 2 * j:2 * j + 2, :])
                g, u, d = col_view(ffn_w_gate[layer]), col_view(ffn_w_up[layer]), row_view(ffn_w_down[layer])
                n = ffn_base(layer)
                load(n, 0, g[:, :, 0:256])
                load(n + 1, 0, u[:, :, 0:256])
                with sp.Fori(0, FP - 2) as i:
                    load(n + 2, i, g[:, :, bass.ds(i * 256 + 256, 256)])
                    load(n + 3, i, d[:, bass.ds(i * 2, 2), :])
                    load(n + 4, i, u[:, :, bass.ds(i * 256 + 256, 256)])
                if layer == LAYERS - 1:
                    sp.wait_ge(pair_used, n)
                    sp.dma_start(final_b, final_gain.partition_broadcast(P)).then_inc(fin_landed, 16)
                last = FP - 1
                load(n + 3 * last - 1, 0, g[:, :, last * 256:])
                load(n + 3 * last, 0, u[:, :, last * 256:])
                load(n + 3 * last + 1, 0, d[:, 2 * last - 2:2 * last, :])
                load(n + 3 * last + 2, 0, d[:, 2 * last:2 * last + 2, :])
            for half in range(2):
                part = slice(half * 512, (half + 1) * 512)
                for tt in (1, 0):
                    sp.wait_ge(fin_ready[tt], half + 1)
                    sp.dma_start(out[0, tt * P:(tt + 1) * P, part], xtok[:, tt, part]).then_inc(out_landed, 16)
            sp.wait_ge(out_landed, 16 * 2 * TT)

        @block_ctx.tensor
        def _(pe):
            def mm(dst, lhsT, rhs, start=False, stop=False):
                return pe.matmul(dst, lhsT, rhs, start=start, stop=stop, skip_group_check=True)

            def split_mm(dst, wh, wl, ah, al, start, stop):
                mm(dst, wh, ah, start=start)
                mm(dst, wh, al)
                return mm(dst, wl, ah, stop=stop)

            def pair_ready(n, i=0):
                pe.wait_ge(hi_ready, n + 1 + 3 * i)
                pe.wait_ge(lo_ready, n + 1 + 3 * i)

            def act_chunk(block, k):
                pe.wait_ge(act_hi_ready, C * block + k + 1)
                pe.wait_ge(act_lo_ready, C * block + k + 1)

            def col_views(n):
                slot = n % SLOTS
                return (w[:, slot, :].rearrange("p (k c) -> p k c", c=256) for w in (w_hi, w_lo))

            def col_tile(n, j, dst, inside=None, at=0):
                wh, wl = col_views(n)
                for k in range(C):
                    if k == at and inside is not None:
                        inside()
                    last = split_mm(dst, wh[:, k, j * P:(j + 1) * P], wl[:, k, j * P:(j + 1) * P],
                                    act_hi[:, k, :], act_lo[:, k, :], j == 0 and k == 0, k == C - 1)
                return last

            def first_pair(n, bank, block, beside=None):
                wh, wl = col_views(n)
                for k in range(C):
                    if n == 0 and k == 0:
                        pe.wait_ge(half_hi, 1)
                        pe.wait_ge(half_lo, 1)
                    if k == (C // 2 if n == 0 else 0):
                        pair_ready(n)
                    act_chunk(block, k)
                    if beside is not None:
                        beside(k)
                    for j in range(2):
                        last = split_mm(ps[:, bank, j * T:(j + 1) * T], wh[:, k, j * P:(j + 1) * P],
                                        wl[:, k, j * P:(j + 1) * P], act_hi[:, k, :], act_lo[:, k, :],
                                        j == 0 and k == 0, k == C - 1)
                last.then_inc(pair_used, 1)

            def second_pair(n, bank, block):
                pair_ready(n)
                col_tile(n, 0, ps[:, bank, 0:T], lambda: norm_sums(block), 4)
                col_tile(n, 1, ps[:, bank, T:2 * T], lambda: norm_broadcast(block), 3).then_inc(pair_used, 1)

            def token_tile(n, tt, dst):
                slot = n % SLOTS
                wh = w_hi[:, slot, :].rearrange("p (k c) -> p k c", c=256)
                wl = w_lo[:, slot, :].rearrange("p (k c) -> p k c", c=256)
                for k in range(C):
                    ah, al = act_hi[:, k, tt * P:(tt + 1) * P], act_lo[:, k, tt * P:(tt + 1) * P]
                    mm(dst, ah, wh[:, k, :], start=(k == 0 and tt == 0))
                    mm(dst, ah, wl[:, k, :])
                    last = mm(dst, al, wh[:, k, :], stop=(k == C - 1))
                return last

            def row_pair(n, ah, al, start=False, chunks=(0, 1)):
                slot = n % SLOTS
                wh = w_hi[:, slot, :].rearrange("p (j c) -> p j c", j=2)
                wl = w_lo[:, slot, :].rearrange("p (j c) -> p j c", j=2)
                for j in chunks:
                    for o in range(C):
                        last = split_mm(acc_tile(o), wh[:, j, o * P:(o + 1) * P], wl[:, j, o * P:(o + 1) * P],
                                        ah[:, j, :], al[:, j, :], start and j == 0 and o % 2 == 0, False)
                return last

            def last_row_pair(n, ah, al, before_last=None):
                slot = n % SLOTS
                wh = w_hi[:, slot, :].rearrange("p (j c) -> p j c", j=2)
                wl = w_lo[:, slot, :].rearrange("p (j c) -> p j c", j=2)
                for o in range(C):
                    if o == C - 1 and before_last is not None:
                        before_last()
                    for j in range(2):
                        last = split_mm(acc_tile(o), wh[:, j, o * P:(o + 1) * P], wl[:, j, o * P:(o + 1) * P],
                                        ah[:, j, :], al[:, j, :], False, j == 1)
                    last.then_inc(acc_done if o < C - 1 else pair_used, 1)

            def norm_sums(block):
                pe.wait_ge(ss_complete, block + 1)
                for tt in range(TT):
                    for half in range(2):
                        last = mm(ps[:, NORM, tt:tt + 1], ss[:, half, tt * P:(tt + 1) * P], ones[:, 0:1],
                                  start=(half == 0), stop=(half == 1))
                last.then_inc(ss_col, 1)

            def norm_broadcast(block):
                pe.wait_ge(diag_ready, block + 1)
                mm(ps[:, NORM, T:2 * T], ones[:, 0:P], diag[:, :], start=True, stop=True).then_inc(rb_ps, 1)

            def keep_warm(products):
                for _ in range(products):
                    mm(ps[:, 0, :], zeros_bf[:, 0:P], zeros_bf[:, :], start=True, stop=True)

            pe.wait_ge(const_set, 1)
            keep_warm(10)
            pe.wait_ge(ident_set, 1)
            pe.wait_ge(rows_landed, 64)
            pe.transpose(ps[:, SPARE, 0:ROWS], rows[:, :], ident[0:ROWS, 0:ROWS]).then_inc(cols_ps, 1)
            pe.wait_ge(x_landed, 32)
            for o in range(C):
                for tt in range(TT):
                    last = pe.transpose(acc_tile(o)[:, tt * P:(tt + 1) * P], xtok[:, tt, o * P:(o + 1) * P], ident)
                last.then_inc(acc_done, 1)

            def mlstm():
                n = mix_base(0)
                pe.wait_ge(gw_hi, 2)
                pe.wait_ge(gw_lo, 2)

                def gates(k):
                    last = split_mm(ps[:, ACC, 0:T], gate_hi[:, k, :], gate_lo[:, k, :],
                                    act_hi[:, k, :], act_lo[:, k, :], k == 0, k == C - 1)
                    if k == C - 1:
                        last.then_inc(gates_ps, 1)

                keep_warm(4)
                for k in range(2):
                    act_chunk(0, k)
                    gates(k)
                keep_warm(4)
                first_pair(n, 0, 0, beside=lambda k: gates(k) if k >= 2 else None)
                norm_sums(0)
                pair_ready(n + 1)
                col_tile(n + 1, 0, ps[:, 1, 0:T], lambda: norm_broadcast(0), 5)
                col_tile(n + 1, 1, ps[:, 1, T:2 * T]).then_inc(pair_used, 1)

                def values(pair, bank):
                    pair_ready(pair)
                    token_tile(pair, 0, ps[:, bank, 0:T])
                    token_tile(pair, 1, ps[:, bank, T:2 * T]).then_inc(pair_used, 1)

                def stage1(h):
                    if h >= 1:
                        pe.wait_ge(ST_ready, h)
                    pe.wait_ge(kbf_ready, 4)
                    pe.wait_ge(select_ready, 1)
                    sel = select[:, h * P:(h + 1) * P]
                    neg_m = gr[:, G_NEG, :]
                    mm(ps[:, 2, 0:T], sel, neg_m, start=True)
                    mm(ps[:, 2, 0:P], ident_bf, kbf[:, 2, :])
                    mm(ps[:, 2, T:T + P], sel, neg_m[:, P:T])
                    mm(ps[:, 2, T:T + P], ident_bf, kbf[:, 2, :], stop=True)
                    pe.wait_ge(m_qk_ready, 2 * (h // 2) + 2)
                    mm(ps[:, 3, 0:T], m_k[:, h, 0:P], m_q[:, h, :], start=True, stop=True)
                    mm(ps[:, 3, T:T + P], m_k[:, h, P:T], m_q[:, h, P:T], start=True, stop=True).then_inc(m_s1, 1)

                def stage2(h):
                    pe.wait_ge(ST_ready, h + 1)
                    pe.wait_ge(m_v_ready, 2 * h + 2)
                    if h >= 1:
                        pe.wait_ge(num_ready, h)
                    for dv in range(2):
                        c0 = h * MDV + dv * P
                        mm(ps[:, 4, dv * T:(dv + 1) * T], v_sb[:, 0, c0:c0 + P], ST[:, 0:T], start=True)
                        mm(ps[:, 4, dv * T + P:(dv + 1) * T], v_sb[:, 1, c0:c0 + P], ST[:, T:T + P], stop=True)
                    mm(ps[:, 5, 2 * h:2 * h + 1], ST[:, 0:P], ones[:, 0:1], start=True, stop=True)
                    mm(ps[:, 5, 2 * h + 1:2 * h + 2], ST[:, P:T], ones[:, 0:1], start=True)
                    mm(ps[:, 5, 2 * h + 1:2 * h + 2], ST[:, T:T + P], ones[:, 0:1], stop=True).then_inc(m_s2, 1)

                def stage3(h):
                    pe.wait_ge(nsq_ready, h + 1)
                    for tt in range(TT):
                        for dv in range(2):
                            last = mm(ps[:, 5, 8 + 2 * h + tt:9 + 2 * h + tt], nsq[:, dv, tt * P:(tt + 1) * P],
                                      ones[:, 0:1], start=(dv == 0), stop=(dv == 1))
                    last.then_inc(m_s3, 1)

                def queries_keys(pair, bank):
                    pair_ready(pair)
                    col_tile(pair, 0, ps[:, bank, 0:T])
                    col_tile(pair, 1, ps[:, bank, T:2 * T]).then_inc(pair_used, 1)

                pe.wait_ge(cols_ready, 1)
                values(n + 2, SPARE)
                pe.wait_ge(R_ready, 1)
                values(n + 3, NORM)
                pe.wait_ge(g_rows, 1)
                for j, row in enumerate((G_C, G_M)):
                    for tt in range(TT):
                        last = mm(ps[:, 5, 32 + 8 * j + 4 * tt:36 + 8 * j + 4 * tt], gr[:, row, tt * P:(tt + 1) * P],
                                  ident[0:MH, 0:MH], start=True, stop=True)
                last.then_inc(gcol_ps, 1)
                pe.wait_ge(m_qk_ready, 2)
                stage1(0)
                queries_keys(n + 4, 0)
                pe.wait_ge(gcol_ready, 1)
                stage2(0)
                stage1(1)
                queries_keys(n + 5, 1)
                stage3(0)
                stage2(1)
                pe.wait_ge(m_v_ready, 4)
                values(n + 6, SPARE)
                stage3(1)
                stage1(2)
                values(n + 7, NORM)
                stage2(2)
                stage1(3)
                pe.wait_ge(m_qk_ready, 4)
                queries_keys(n + 8, 0)
                stage3(2)
                stage2(3)
                queries_keys(n + 9, 1)
                stage3(3)
                pe.wait_ge(o_scaled, 1)
                queries_keys(n + 10, 0)
                pe.wait_ge(m_diag_ready, 1)
                pe.wait_ge(m_v_ready, 2 * MH)
                for g in range(2):
                    last = mm(ps[:, (SPARE, NORM)[g], :], ones[:, 0:P], m_diag[:, 2 * g:2 * g + 2, :].rearrange("p h t -> p (h t)"),
                              start=True, stop=True)
                last.then_inc(m_fb, 1)
                pe.wait_ge(o_scaled, 2)
                queries_keys(n + 11, 1)

            def attention(layer):
                moba = layer == 1
                n0 = mix_base(layer)
                G0 = 0 if moba else GROUPS
                block = 2 * layer

                def scores(g, banks=(2, 4)):
                    pe.wait_ge(qk_ready, 2 * g + 2 * G0 + 2)
                    for h in range(4):
                        if h == 2 and banks is LAST_BANKS:
                            pe.wait_ge(v_ready, 2 * (G0 + GROUPS))
                            pe.wait_ge(mix_hi_ready, C * layer + 2 * GROUPS - 2)
                            pe.wait_ge(mix_lo_ready, C * layer + 2 * GROUPS - 2)
                        rows_ = slice(DH * (h % 2), DH * (h % 2) + DH)
                        q, k = q_f[rows_, h // 2, :], k_f[rows_, h // 2, :]
                        b = banks[h // 2] + h % 2
                        if moba:
                            mm(ps[:, b, 0:P], q[:, 0:P], k[:, 0:P], start=True)
                            mm(ps[:, b, 0:P], ident_bf, kbf[:, 1, :], stop=True)
                            mm(ps[:, b, P:384], q[:, P:T], k[:, :], start=True)
                            last = mm(ps[:, b, T:384], ident_bf, kbf[:, 1, :], stop=True)
                        else:
                            mm(ps[:, b, 0:T], k[:, 0:P], q[:, :], start=True)
                            mm(ps[:, b, 0:P], ident_bf, kbf[:, 3, :])
                            mm(ps[:, b, T:384], k[:, P:T], q[:, P:T])
                            last = mm(ps[:, b, T:384], ident_bf, kbf[:, 3, :])
                        if h % 2:
                            last.then_inc(scores_done, 1)

                def stage2(g, banks=(2, 4)):
                    for half in range(2):
                        if not moba:
                            pe.wait_ge(exact_ready, 2)
                        pe.wait_ge(prob_ready, 2 * g + 2 * G0 + half + 1)
                        for h in (2 * half, 2 * half + 1):
                            b = banks[half] + h % 2
                            if moba:
                                pe.transpose(ps[:, b, 0:P], prob[:, h, 0:P], ident)
                                pe.transpose(ps[:, b, P:T], prob[:, h, P:T], ident)
                                last = pe.transpose(ps[:, b, T:384], prob[:, h, T:384], ident)
                            else:
                                for part in (soft_hi, soft_lo):
                                    mm(ps[:, b, 0:T], suffix[:, :], part[:, h, 0:T])
                                    mm(ps[:, b, P:T], minus[:, :], part[:, h, T:384])
                                    last = mm(ps[:, b, T:384], suffix[:, :], part[:, h, T:384],
                                              stop=part is soft_lo)
                        last.then_inc(stage2_done, 1)

                def stage3(g, bank=NORM):
                    pe.wait_ge(probt_dve if moba else probt_act, (g + 1) if moba else 2 * g + 2 + GROUPS)
                    if moba:
                        pe.wait_ge(probt_act, g + 1)
                    pe.wait_ge(v_ready, 2 * g + 2 * G0 + 2)
                    pe.wait_ge(mix_hi_ready, 2 * g + C * layer)
                    pe.wait_ge(mix_lo_ready, 2 * g + C * layer)
                    for h in range(4):
                        dst = ps[DH * (h % 2):DH * (h % 2) + DH, bank, (h // 2) * T:(h // 2 + 1) * T]
                        mm(dst, v_sb[:, 0, h * DH:(h + 1) * DH], prob_t[:, h, 0:T], start=True)
                        last = mm(dst[:, P:T], v_sb[:, 1, h * DH:(h + 1) * DH], prob_t[:, h, T:384], stop=True)
                    last.then_inc(pv_done, 1)

                def project(g, part, bank, between=None):
                    n = n0 + part
                    pair_ready(n, g)
                    col_tile(n, 0, ps[:, bank, 0:T])
                    if between is not None:
                        between()
                    col_tile(n, 1, ps[:, bank, T:2 * T]).then_inc(pair_used, 1)

                def permute(g, j):
                    if moba:
                        pe.wait_ge(exact_ready, 2)
                        pe.wait_ge(qk_lo_ready, 2 * g + j + 1)
                        mm(ps[:, j, :], perm[:, :], qk_hi[:, j].rearrange("p j t -> p (j t)"), start=True)
                        mm(ps[:, j, :], perm[:, :], qk_lo[:, j].rearrange("p j t -> p (j t)"), stop=True).then_inc(perm_done, 1)

                def project_v(g, permutes=(1,)):
                    n = n0 + 2
                    pair_ready(n, g)
                    token_tile(n, 0, ps[:, SPARE, 0:T])
                    for j in permutes:
                        permute(g, j)
                    token_tile(n, 1, ps[:, SPARE, T:2 * T]).then_inc(pair_used, 1)

                first_pair(n0, 0, block)
                second_pair(n0 + 1, 1, block)
                project_v(0, permutes=(0, 1))
                with pe.Fori(0, GROUPS - 1) as g:
                    scores(g)
                    project(g + 1, 0, 0)
                    project(g + 1, 1, 1, between=lambda: stage2(g))
                    permute(g + 1, 0)
                    stage3(g)
                    project_v(g + 1)
                scores(GROUPS - 1, LAST_BANKS)
                wout(layer, 0)
                wout(layer, 1, (0,))
                stage2(GROUPS - 1, LAST_BANKS)
                wout(layer, 1, (1,))
                stage3(GROUPS - 1, 0)
                wout(layer, 2)
                wout(layer, 3)

            def conv():
                n0 = mix_base(2)
                def body(c, first):
                    for part, bank in enumerate((SPARE, 0, 1)):
                        if first and part == 0:
                            first_pair(n0, bank, 4)
                            continue
                        if first and part == 1:
                            second_pair(n0 + 1, bank, 4)
                            continue
                        if not first:
                            pe.wait_ge(conv_evac, 3 * c + part - 2)
                        pair_ready(n0 + part, c)
                        col_tile(n0 + part, 0, ps[:, bank, 0:T])
                        col_tile(n0 + part, 1, ps[:, bank, T:2 * T]).then_inc(pair_used, 1)
                body(0, True)
                with pe.Fori(1, GROUPS) as c:
                    body(c, False)

            def wout(layer, p, chunks=(0, 1)):
                n = wout_base(layer) + p
                pe.wait_ge(mix_hi_ready, C * layer + 2 * p + 2)
                pe.wait_ge(mix_lo_ready, C * layer + 2 * p + 2)
                pair_ready(n)
                ah, al = mix_hi[:, 2 * p:2 * p + 2, :], mix_lo[:, 2 * p:2 * p + 2, :]
                if p < 3:
                    last = row_pair(n, ah, al, start=(p == 0), chunks=chunks)
                    if 1 in chunks:
                        last.then_inc(pair_used, 1)
                else:
                    last_row_pair(n, ah, al)

            def ffn(layer):
                n = ffn_base(layer)
                block = 2 * layer + 1
                t0 = FP * layer

                def tiles(pair, i, bank, hidden):
                    pair_ready(pair, i)
                    pe.wait_ge((g_scaled, u_scaled)[bank], hidden)
                    col_tile(pair, 0, ps[:, bank, 0:T])
                    col_tile(pair, 1, ps[:, bank, T:2 * T]).then_inc(pair_used, 1)

                def down(pair, i, hidden, start=False):
                    pe.wait_ge(h_hi_ready, hidden)
                    pe.wait_ge(h_lo_ready, hidden)
                    pair_ready(pair, i)
                    row_pair(pair, h_hi[:, 0], h_lo[:, 0], start=start).then_inc(pair_used, 1)

                first_pair(n, 0, block)
                second_pair(n + 1, 1, block)
                tiles(n + 2, 0, 0, t0 + 1)
                down(n + 3, 0, t0 + 1, start=True)
                tiles(n + 4, 0, 1, t0 + 1)
                with pe.Fori(0, FP - 3) as i:
                    tiles(n + 5, i, 0, i + t0 + 2)
                    down(n + 6, i, i + t0 + 2)
                    tiles(n + 7, i, 1, i + t0 + 2)
                last = FP - 1
                tiles(n + 3 * last - 1, 0, 0, t0 + last)
                tiles(n + 3 * last, 0, 1, t0 + last)
                down(n + 3 * last + 1, 0, t0 + last)
                pe.wait_ge(h_hi_ready, t0 + FP)
                pe.wait_ge(h_lo_ready, t0 + FP)
                pair_ready(n + 3 * last + 2)
                last_row_pair(n + 3 * last + 2, h_hi[:, 1], h_lo[:, 1],
                              (lambda: token_major(0)) if layer == LAYERS - 1 else None)

            def token_major(half):
                for o in range(4 * half, 4 * half + 4):
                    pe.wait_ge(resid_ready, 4 * 8 + o // 2 + 1)
                    for tt in range(TT):
                        last = pe.transpose(ps[:, FINAL_BANKS[tt][half], (o % 4) * P:(o % 4 + 1) * P],
                                            resid[:, o, tt * P:(tt + 1) * P], ident)
                last.then_inc(fin_ps, 1)

            for layer in range(LAYERS):
                if layer == 0:
                    mlstm()
                elif layer == 2:
                    conv()
                else:
                    attention(layer)
                if layer in (0, 2):
                    for p in range(4):
                        wout(layer, p)
                ffn(layer)
            token_major(1)

        @block_ctx.scalar
        def _(act):
            def round_pair(n, i=0):
                if n >= PAIRS:
                    return
                slot, lap = n % SLOTS, n // SLOTS
                act.wait_ge(raw_landed[slot], 16 * (lap + 1) + 16 * i)
                if n >= SLOTS:
                    act.wait_ge(pair_used, n - 2 + 3 * i)
                act.activation(w_hi[:, slot, :], w_raw[:, slot, :], ACT.Copy).then_inc(hi_ready, 1)

            def finish(block):
                if block > 0:
                    act.preload_act_table_set("sqrt_and_others")
                for b in range(C // 2):
                    act.wait_ge(resid_ready, 4 * block + b + 1)
                    for o in (2 * b, 2 * b + 1):
                        act.activation(act_hi[:, o, :], resid[:, o, :], ACT.Copy, scale=gain_col[block][o])\
                           .then_inc(act_hi_ready, 1)
                    if block == 0 and b == 0:
                        act.wait_ge(half_landed, 16)
                        act.activation(w_hi[:, 0, 0:1024], w_raw[:, 0, 0:1024], ACT.Copy).then_inc(half_hi, 1)
                    if block == 0 and b == 1:
                        act.wait_ge(raw_landed[0], 16)
                        act.activation(w_hi[:, 0, 1024:], w_raw[:, 0, 1024:], ACT.Copy).then_inc(hi_ready, 1)
                    behind = 1 - block % 2
                    if 0 <= b - behind <= 1:
                        a = b - behind
                        if a == 0 and block > 0:
                            act.wait_ge(ss_complete, block)
                        act.activation(sq[:, a], resid[:, 2 * a:2 * a + 2, :], ACT.Square).then_inc(sq_ready, 1)

            def norm_root(block):
                act.wait_ge(ss_col, block + 1)
                act.activation(rms_sd[:, :], ps[:, NORM, 0:TT], ACT.Sqrt, bias=eps[:, :], scale=1.0 / D)\
                   .then_inc(sd_ready, 1)

            act.dma_start(rows[ROW_GAIN:ROW_GAIN + 64, :], norm_gains.rearrange("l b (c p) -> (l b c) p", p=P))\
               .then_inc(rows_landed, 16)
            act.dma_start(rows[ROW_HEAD:ROW_HEAD + 8, :], mlstm_head_gain.rearrange("a (c p) -> (a c) p", p=P))\
               .then_inc(rows_landed, 16)
            with nc.allow_non_contiguous_dma(reason="eight gate columns"):
                act.dma_start(gate_raw[:, :, :], col_view(mlstm_w_in[0])[:, :, 3 * D:3 * D + 2 * MH]).then_inc(gate_landed, 16)
                act.dma_start(bias_i[:, :], mlstm_b_gate[0, 0:MH].rearrange("(h a) -> h a", a=1)).then_inc(bias_landed, 16)
                act.dma_start(bias_f[:, :], mlstm_b_gate[0, MH:2 * MH].rearrange("(h a) -> h a", a=1)).then_inc(bias_landed, 16)
            act.preload_act_table_set("sqrt_and_others")
            act.wait_ge(gate_landed, 16)
            act.wait_ge(gw_zero, 1)
            act.activation(gate_hi[:, :, 0:MH], gate_raw[:, :, 0:MH], ACT.Copy).then_inc(gw_hi, 1)
            act.activation(gate_hi[:, :, 32:32 + MH], gate_raw[:, :, MH:2 * MH], ACT.Copy).then_inc(gw_hi, 1)
            act.wait_ge(cols_ready, 1)
            act.wait_ge(const_set, 1)
            finish(0)
            round_pair(1)
            round_pair(2)
            norm_root(0)

            def mlstm():
                n = mix_base(0)
                act.preload_act_table_set("natural_log_exp_and_others")
                round_pair(n + 3)
                act.wait_ge(k_landed, 16)
                act.wait_ge(kbf_ready, 5)
                act.activation(perm[:, :], perm_raw, ACT.Copy).then_inc(exact_ready, 1)
                act.activation(suffix[:, :], suffix_raw, ACT.Copy).then_inc(exact_ready, 1)
                act.wait_ge(f_scaled, 1)
                act.wait_ge(bias_landed, 32)
                act.activation(gr[:, G_F, :], gate_sc[32:32 + MH, :], ACT.Identity, bias=bias_f[:, :]).then_inc(f_moved, 1)
                act.activation(gr[:, G_I, :], gate_sc[0:MH, :], ACT.Identity, bias=bias_i[:, :]).then_inc(f_moved, 1)
                act.wait_ge(f_moved, 2)
                act.activation(gr[:, G_LN, :], gr[:, G_F, :], ACT.Abs).then_inc(f_moved, 1)
                act.wait_ge(f_moved, 3)
                act.activation(gr[:, G_LN, :], gr[:, G_LN, :], ACT.Exp, scale=-1.0).then_inc(f_moved, 1)
                act.wait_ge(f_moved, 4)
                act.activation(gr[:, G_LN, :], gr[:, G_LN, :], ACT.Ln, bias=1.0).then_inc(f_logs, 1)
                round_pair(n + 4)

                def value(h):
                    act.wait_ge(pair_used, n + (3, 4, 7, 8)[h])
                    act.wait_ge(diag_ready, 1)
                    for tt in range(TT):
                        act.activation(v_sb[:, tt, h * MDV:(h + 1) * MDV], flat((SPARE, NORM)[h % 2])[:, tt, :],
                                       ACT.Copy, scale=rms_col[:, tt:tt + 1]).then_inc(m_v_ready, 1)

                def weights(h):
                    act.wait_ge(m_s1, h + 1)
                    act.wait_ge(gcol_ready, 1)
                    for s in range(2):
                        a, b = ((0, T), (T, 384))[s]
                        last = act.activation(E[:, a:b], ps[:, 2, a:b], ACT.Exp, bias=gcol[:, 4 * s + h:4 * s + h + 1])
                    last.then_inc(E_ready, 1)

                value(0)
                round_pair(n + 5)
                value(1)
                round_pair(n + 6)
                act.wait_ge(gcol_ready, 1)
                act.activation(expnegm[:, :], gcol[:, 8:16], ACT.Exp, scale=-1.0).then_inc(expm_ready, 1)
                weights(0)
                round_pair(n + 7)
                weights(1)
                round_pair(n + 8)
                value(2)
                round_pair(n + 9)
                weights(2)
                value(3)
                round_pair(n + 10)
                weights(3)
                round_pair(n + 11)
                round_pair(n + 12)
                act.wait_ge(m_var, 1)
                act.activation(fc[:, 5, :], fc[:, 4, :], ACT.Sqrt, bias=eps[:, :], scale=1.0 / MDV).then_inc(m_sd, 1)

                def out_gate(j):
                    act.wait_ge(o_scaled, j + 1)
                    act.activation(o_sc[:, 2 * j:2 * j + 2, :], o_sc[:, 2 * j:2 * j + 2, :], ACT.Sigmoid).then_inc(o_sig, 1)

                def mixed(h):
                    act.wait_ge(m_mix, h + 1)
                    act.activation(mix_hi[:, 2 * h:2 * h + 2, :], mix32[:, h % 2], ACT.Copy).then_inc(mix_hi_ready, 2)

                for j in range(3):
                    out_gate(j)
                round_pair(n + 13)
                mixed(0)
                mixed(1)
                out_gate(3)
                mixed(2)
                round_pair(n + 14)
                mixed(3)
                mix_tail(0)

            def mix_tail(layer):
                n = wout_base(layer)
                round_pair(n + 3)
                round_pair(n + 4)
                round_pair(n + 5)
                finish(2 * layer + 1)
                round_pair(n + 6)
                norm_root(2 * layer + 1)

            def attention(layer):
                moba = layer == 1
                n0 = mix_base(layer)
                G0 = 0 if moba else GROUPS

                if not moba:
                    act.preload_act_table_set("natural_log_exp_and_others")

                def raw_copy(g, j):
                    if moba:
                        act.wait_ge(pair_used, n0 + j + 1 + 3 * g)
                        act.activation(qk_hi[:, j], flat(j), ACT.Copy).then_inc(qk_raw_ready, 1)

                def value(g, tt):
                    act.wait_ge(pair_used, n0 + 3 + 3 * g)
                    act.activation(v_sb[:, tt, 0:T], flat(SPARE)[:, tt, :], ACT.Copy, scale=rms_col[:, tt:tt + 1])\
                       .then_inc(v_ready, 1)

                def soft1(g, banks=(2, 4)):
                    for half in range(2):
                        hs = slice(2 * half, 2 * half + 2)
                        if moba:
                            act.wait_ge(nmax_ready, 2 * g + half + 1)
                            for h in (2 * half, 2 * half + 1):
                                for tb in range(2):
                                    a, b = ((0, P), (P, 384))[tb]
                                    c = 4 * half + 2 * tb + h % 2
                                    last = act.activation(prob[:, h, a:b], ps[:, banks[half] + h % 2, a:b], ACT.Exp,
                                                          bias=nmx[:, c:c + 1], accum_out=rsum[:, c:c + 1])
                            last.then_inc(exp_done, 1)
                        else:
                            z = ps[:, banks[half]:banks[half] + 2, 0:384]
                            act.wait_ge(scores_done, 2 * g + 2 * G0 + half + 1)
                            act.activation(sp_a[:, hs, :], z, ACT.Abs).then_inc(softplus_step, 1)
                            act.wait_ge(softplus_step, 4 * g + 2 * half + 1)
                            act.activation(sp_a[:, hs, :], sp_a[:, hs, :], ACT.Exp, scale=-1.0).then_inc(softplus_step, 1)
                            act.wait_ge(softplus_step, 4 * g + 2 * half + 2)
                            act.activation(sp_a[:, hs, :], sp_a[:, hs, :], ACT.Ln, bias=1.0).then_inc(log_ready, 1)
                    if not moba:
                        for half in range(2):
                            hs = slice(2 * half, 2 * half + 2)
                            act.wait_ge(soft_ready, 2 * g + half + 1)
                            act.activation(soft_hi[:, hs, :], prob[:, hs, :], ACT.Copy).then_inc(soft_hi_ready, 1)

                def soft2(g, banks=(2, 4)):
                    for half in range(2):
                        hs = slice(2 * half, 2 * half + 2)
                        if moba and half == 0:
                            continue
                        act.wait_ge(stage2_done, 2 * g + 2 * G0 + half + 1)
                        act.activation(prob_t[:, hs, :], ps[:, banks[half]:banks[half] + 2, 0:384],
                                       ACT.Copy if moba else ACT.Exp).then_inc(probt_act, 1)

                def mixed(g, bank=NORM):
                    act.wait_ge(pv_done, g + G0 + 1)
                    act.activation(mix_hi[:, bass.ds(2 * g, 2), :] if not isinstance(g, int) else mix_hi[:, 2 * g:2 * g + 2, :],
                                   flat(bank), ACT.Copy).then_inc(mix_hi_ready, 2)

                raw_copy(0, 0)
                round_pair(n0 + 3)
                act.wait_ge(diag_ready, 2 * layer + 1)
                raw_copy(0, 1)
                round_pair(n0 + 4)
                value(0, 0)
                value(0, 1)
                with act.Fori(0, GROUPS - 1) as g:
                    soft1(g)
                    round_pair(n0 + 5, g)
                    raw_copy(g + 1, 0)
                    round_pair(n0 + 6, g)
                    soft2(g)
                    raw_copy(g + 1, 1)
                    round_pair(n0 + 7, g)
                    mixed(g)
                    value(g + 1, 0)
                    value(g + 1, 1)
                soft1(GROUPS - 1, LAST_BANKS)
                round_pair(n0 + 14)
                soft2(GROUPS - 1, LAST_BANKS)
                mixed(GROUPS - 1, 0)
                mix_tail(layer)

            def conv():
                n0 = mix_base(2)

                def body(c, first):
                    g = c - 1 if not first else 0
                    act.wait_ge(pair_used, n0 + 1 + 3 * c)
                    base = 3 if first else 6
                    round_pair(n0 + base, g)
                    act.wait_ge(pair_used, n0 + 2 + 3 * c)
                    round_pair(n0 + base + 1, g)
                    round_pair(n0 + base + 2, g)
                    act.wait_ge(z_ready, c + 1)
                    for j in range(2):
                        w2 = cols[:, ROW_CONV + 16 + j:ROW_CONV + 17 + j] if first else \
                            cols[:, bass.ds(2 * c + (ROW_CONV + 16 + j), 1)]
                        act.activation(y_sb[:, j, :], z_pad[:, j, 2:T + 2], ACT.Copy, scale=w2).then_inc(y_act, 1)
                    act.wait_ge(cmix_ready, c + 1)
                    dst = mix_hi[:, 0:2, :] if first else mix_hi[:, bass.ds(2 * c, 2), :]
                    act.activation(dst, mix32[:, 0], ACT.Copy).then_inc(mix_hi_ready, 2)
                body(0, True)
                with act.Fori(1, GROUPS) as c:
                    body(c, False)
                mix_tail(2)

            def ffn(layer):
                n = ffn_base(layer)
                t0 = FP * layer
                act.preload_act_table_set("silu_and_others")
                if layer == 0:
                    act.wait_ge(ang_ready, 1)
                    act.activation(ang[:, 2:4, :], ang[:, 2:4, :], ACT.Sin).then_inc(trig_ready, 1)

                def silu(t):
                    act.wait_ge(g_scaled, t + 1)
                    act.activation(sil[:, :, :], g_sc[:, :, :], ACT.Silu).then_inc(silu_done, 1)

                def high(t, set_):
                    act.wait_ge(hid_ready, t + 1)
                    act.activation(h_hi[:, set_], hid[:, :, :], ACT.Copy).then_inc(h_hi_ready, 1)

                round_pair(n + 3)
                silu(t0)
                high(t0, 0)
                round_pair(n + 4)
                with act.Fori(0, FP - 2) as i:
                    silu(i + t0 + 1)
                    round_pair(n + 5, i)
                    round_pair(n + 6, i)
                    high(i + t0 + 1, 0)
                    round_pair(n + 7, i)
                t, m = t0 + FP - 1, n + 3 * FP
                silu(t)
                round_pair(m - 1)
                high(t, 1)
                round_pair(m)
                if layer < LAYERS - 1:
                    round_pair(m + 1)
                    finish(2 * layer + 2)
                    round_pair(m + 2)
                    norm_root(2 * layer + 2)

            for layer in range(LAYERS):
                if layer == 0:
                    mlstm()
                elif layer == 2:
                    conv()
                else:
                    attention(layer)
                ffn(layer)
            for half in range(2):
                act.wait_ge(fin_ps, half + 1)
                for tt in range(TT):
                    if tt == 1:
                        act.wait_ge(fin_gained, 2 * half + 1)
                    if half == 1:
                        act.wait_ge(fin_squared, tt + 1)
                    act.activation(sq[:, tt], flat(FINAL_BANKS[tt][half]), ACT.Square,
                                   accum_out=fin_sums[:, half, tt:tt + 1]).then_inc(fin_squared, 1)
            act.wait_ge(fin_summed, 1)
            act.activation(rms_sd[:, :], fin_sums[:, 0, :], ACT.Sqrt, bias=eps[:, :], scale=1.0 / D).then_inc(sd_ready, 1)
            act.wait_ge(fin_rms, 1)
            act.wait_ge(fin_gained, 2 * TT)
            for part in (slice(0, 512), slice(512, D)):
                act.activation(xtok[:, 0, part], xtok[:, 0, part], ACT.Copy, scale=rms_col[:, 0:1]).then_inc(fin_ready[0], 1)

        @block_ctx.vector
        def _(dve):
            steps = [0]

            def link(ins):
                steps[0] += 1
                ins.then_inc(dve_step, 1)
                dve.wait_ge(dve_step, steps[0])

            def low_pair(n, i=0):
                if n >= PAIRS:
                    return
                slot = n % SLOTS
                dve.wait_ge(hi_ready, n + 1 + 3 * i)
                dve.tensor_tensor(w_lo[:, slot, :], w_raw[:, slot, :], w_hi[:, slot, :].bitcast(F32), ALU.subtract)\
                   .then_inc(lo_ready, 1)

            def act_low(block, chunks):
                for o in chunks:
                    dve.wait_ge(act_hi_ready, C * block + o + 1)
                    dve.scalar_tensor_tensor(out=act_lo[:, o, :], in0=resid[:, o, :], scalar=gain_col[block][o],
                                             in1=act_hi[:, o, :].bitcast(F32), op0=ALU.mult, op1=ALU.subtract)\
                       .then_inc(act_lo_ready, 1)

            def last_squares(block):
                r, own = resid[:, C - 2:C, :], mlt[:, 0]
                dve.tensor_tensor(own, r, r, ALU.mult).then_inc(own_squared, 1)
                dve.wait_ge(own_squared, block + 1)
                dve.wait_ge(sq_ready, 2 * block + 2)
                dve.tensor_tensor(sq[:, 1], sq[:, 1], own, ALU.add).then_inc(last_squared, 1)

            def residual(block, b):
                dve.wait_ge(*acc_wait(block, 2 * b))
                r = resid[:, 2 * b:2 * b + 2, :]
                if block == 0:
                    ins = dve.tensor_copy(r, flat(ACC + b))
                else:
                    ins = dve.tensor_tensor(r, r, flat(ACC + b), ALU.add)
                ins.then_inc(resid_ready, 1)

            def finish(block):
                for b in range(C // 2):
                    residual(block, b)
                    if b >= 1:
                        act_low(block, (2 * b - 2, 2 * b - 1))
                act_low(block, (C - 2, C - 1))
                last_squares(block)

            def norm_diag(block):
                dve.wait_ge(sd_ready, block + 1)
                link(dve.reciprocal(rms_col[:, :], rms_sd[:, :]))
                for tt in range(TT):
                    last = dve.tensor_scalar(diag[:, tt * P:(tt + 1) * P], ident, rms_col[:, tt:tt + 1], None, ALU.mult)
                last.then_inc(diag_ready, 1)

            def norm_row(block):
                dve.wait_ge(rb_ps, block + 1)
                dve.tensor_copy(R_sb[:, :], ps[:, NORM, T:2 * T]).then_inc(R_ready, 1)
                dve.wait_ge(R_ready, block + 1)

            def trig_angles():
                dve.wait_ge(pos_landed, 16)
                inv = cols[:, ROW_ROPE:ROW_ROPE + 1]
                a, n, c, s = (ang[:, j, :] for j in range(4))
                link(dve.tensor_copy(a, ang[:, 1, :].bitcast(I32)))
                link(dve.tensor_scalar(a, a, inv, None, ALU.mult))
                link(dve.tensor_scalar(n, a, 1.0 / TWO_PI, ROUNDER, ALU.mult, ALU.add))
                link(dve.tensor_scalar(n, n, ROUNDER, None, ALU.subtract))
                for part in (TWO_PI_A, TWO_PI_B, TWO_PI_C):
                    link(dve.scalar_tensor_tensor(out=a, in0=n, scalar=-part, in1=a, op0=ALU.mult, op1=ALU.add))
                link(dve.tensor_scalar(s, a, PI_F, -PI_F, ALU.min, ALU.max))
                link(dve.tensor_scalar(n, a, math.pi / 2, -TWO_PI, ALU.is_gt, ALU.mult))
                link(dve.scalar_tensor_tensor(out=c, in0=a, scalar=math.pi / 2, in1=n, op0=ALU.add, op1=ALU.add))
                dve.tensor_scalar(c, c, PI_F, -PI_F, ALU.min, ALU.max).then_inc(ang_ready, 1)

            def trig_tables():
                c, s = ang[:, 2, :], ang[:, 3, :]
                sign, rot = cols[:, ROW_ROPE + 1:ROW_ROPE + 2], cols[:, ROW_ROPE + 2:ROW_ROPE + 3]
                dve.wait_ge(trig_ready, 1)
                link(dve.tensor_scalar(cos_t[:, :], c, -1.0, rot, ALU.add, ALU.mult))
                link(dve.tensor_scalar(cos_t[:, :], cos_t[:, :], 1.0, None, ALU.add))
                link(dve.tensor_scalar(sin_t[:, :], s, sign, None, ALU.mult))

            dve.memset(ones[:, :], 1.0)
            dve.memset(minus[:, :].bitcast(F32), -1.0)
            dve.memset(eps[:, :], EPS)
            dve.memset(zeros_bf[:, :], 0.0).then_inc(const_set, 1)
            dve.wait_ge(ident_set, 1)
            for h in range(MH):
                last = dve.tensor_copy(select[:, h * P:(h + 1) * P], ident[0:MH, h:h + 1].to_broadcast([MH, P]))
            last.then_inc(select_ready, 1)
            dve.wait_ge(cols_ps, 1)
            dve.tensor_copy(cols[:, :], ps[:, SPARE, 0:ROWS]).then_inc(cols_ready, 1)
            dve.wait_ge(cols_ready, 1)
            for a, w in enumerate((0, 32)):
                dve.wait_ge(gw_hi, a + 1)
                dve.tensor_tensor(gate_lo[:, :, w:w + MH], gate_raw[:, :, a * MH:(a + 1) * MH],
                                  gate_hi[:, :, w:w + MH].bitcast(F32), ALU.subtract).then_inc(gw_lo, 1)
            residual(0, 0)
            residual(0, 1)
            act_low(0, (0, 1))
            def low_half(half):
                part = slice(half * 1024, (half + 1) * 1024)
                dve.wait_ge((half_hi, hi_ready)[half], 1)
                dve.tensor_tensor(w_lo[:, 0, part], w_raw[:, 0, part], w_hi[:, 0, part].bitcast(F32), ALU.subtract)\
                   .then_inc((half_lo, lo_ready)[half], 1)

            residual(0, 2)
            low_half(0)
            act_low(0, (2, 3))
            residual(0, 3)
            low_half(1)
            act_low(0, range(4, C))
            last_squares(0)
            low_pair(1)
            norm_diag(0)
            low_pair(2)

            def mlstm():
                n = mix_base(0)
                norm_row(0)
                dve.wait_ge(gates_ps, 1)
                dve.tensor_tensor(gate_sc[0:32 + MH, :], ps[0:32 + MH, ACC, 0:T], R_sb[0:32 + MH, :], ALU.mult)\
                   .then_inc(f_scaled, 1)
                low_pair(n + 3)

                def scale_qk(j, dst, bank, used):
                    dve.wait_ge(pair_used, used)
                    dve.tensor_tensor(dst, flat(bank), bcast(R_sb[:, :], 2), ALU.mult).then_inc(m_qk_ready, 1)

                scale_qk(0, m_q[:, 0:2, :], 0, n + 1)
                scale_qk(1, m_k[:, 0:2, :], 1, n + 2)
                dve.wait_ge(f_logs, 1)
                link(dve.scalar_tensor_tensor(out=gr[:, G_LS, :], in0=gr[:, G_F, :], scalar=0.0, in1=gr[:, G_LN, :],
                                              op0=ALU.min, op1=ALU.subtract))
                link(dve.tensor_tensor_scan(gr[:, G_B, :], ones[0:MH, :], gr[:, G_LS, :], 0.0, ALU.mult, ALU.add))
                link(dve.tensor_tensor(gr[:, G_C, :], gr[:, G_I, :], gr[:, G_B, :], ALU.subtract))
                link(dve.tensor_tensor_scan(gr[:, G_MAX, :], gr[:, G_C, :], gr[:, G_C, :], 0.0, ALU.max, ALU.max))
                link(dve.tensor_tensor(gr[:, G_M, :], gr[:, G_B, :], gr[:, G_MAX, :], ALU.add))
                dve.tensor_scalar(gr[:, G_NEG, :], gr[:, G_MAX, :], -1.0, None, ALU.mult).then_inc(g_rows, 1)
                low_pair(n + 4)
                dve.wait_ge(gcol_ps, 1)
                dve.tensor_copy(gcol[:, :], ps[:, 5, 32:48]).then_inc(gcol_ready, 1)

                def weigh(h):
                    dve.wait_ge(E_ready, h + 1)
                    dve.scalar_tensor_tensor(out=ST[:, :], in0=ps[:, 3, 0:384], scalar=MDK ** -0.5, in1=E[:, :],
                                             op0=ALU.mult, op1=ALU.mult).then_inc(ST_ready, 1)

                def numer(h):
                    dve.wait_ge(m_s2, h + 1)
                    dve.tensor_copy(nums[:, h], flat(4)).then_inc(num_ready, 1)

                weigh(0)
                low_pair(n + 5)
                trig_angles()
                low_pair(n + 6)
                numer(0)
                weigh(1)
                scale_qk(2, m_q[:, 2:4, :], 0, n + 5)
                low_pair(n + 7)
                numer(1)
                scale_qk(3, m_k[:, 2:4, :], 1, n + 6)
                low_pair(n + 8)
                low_pair(n + 9)
                weigh(2)
                low_pair(n + 10)
                numer(2)
                weigh(3)

                def scale_o(j):
                    dve.wait_ge(pair_used, n + 9 + j)
                    dve.tensor_tensor(o_sc[:, 2 * j:2 * j + 2, :], flat(j % 2), bcast(R_sb[:, :], 2), ALU.mult)\
                       .then_inc(o_scaled, 1)
                scale_o(0)
                low_pair(n + 11)
                numer(3)
                scale_o(1)
                dve.wait_ge(m_s3, MH)
                dve.wait_ge(expm_ready, 1)
                link(dve.tensor_copy(fc[:, 6, :], ps[:, 5, 0:8]))
                link(dve.scalar_tensor_tensor(out=fc[:, 0, :], in0=fc[:, 6, :], scalar=-1.0, in1=fc[:, 6, :],
                                              op0=ALU.mult, op1=ALU.max))
                link(dve.tensor_tensor(fc[:, 1, :].rearrange("p (h t) -> p t h", t=2),
                                       fc[:, 0, :].rearrange("p (h t) -> p t h", t=2),
                                       expnegm[:, :].rearrange("p (t h) -> p t h", t=2), ALU.max))
                link(dve.reciprocal(fc[:, 2, :], fc[:, 1, :]))
                link(dve.tensor_tensor(fc[:, 3, :], fc[:, 2, :], fc[:, 2, :], ALU.mult))
                dve.tensor_tensor(fc[:, 4, :], ps[:, 5, 8:16], fc[:, 3, :], ALU.mult).then_inc(m_var, 1)
                dve.wait_ge(m_sd, 1)
                link(dve.reciprocal(fc[:, 6, :], fc[:, 5, :]))
                link(dve.tensor_tensor(fc[:, 7, :], fc[:, 6, :], fc[:, 2, :], ALU.mult))
                for h in range(MH):
                    for tt in range(TT):
                        last = dve.tensor_scalar(m_diag[:, h, tt * P:(tt + 1) * P], ident,
                                                 fc[:, 7, 2 * h + tt:2 * h + tt + 1], None, ALU.mult)
                last.then_inc(m_diag_ready, 1)
                scale_o(2)
                dve.wait_ge(m_fb, 1)

                def factor(h):
                    if h >= 2:
                        dve.wait_ge(m_mix, h - 1)
                    for dv in range(2):
                        last = dve.scalar_tensor_tensor(
                            out=mlt[:, h % 2, dv, :], in0=nums[:, h, dv, :],
                            scalar=cols[:, ROW_HEAD + 2 * h + dv:ROW_HEAD + 2 * h + dv + 1],
                            in1=ps[:, (SPARE, NORM)[h // 2], (h % 2) * T:(h % 2 + 1) * T], op0=ALU.mult, op1=ALU.mult)
                    last.then_inc(m_t_ready, 1)

                def low(h):
                    dve.wait_ge(mix_hi_ready, 2 * h + 2)
                    dve.tensor_tensor(mix_lo[:, 2 * h:2 * h + 2, :], mix32[:, h % 2],
                                      mix_hi[:, 2 * h:2 * h + 2, :].bitcast(F32), ALU.subtract).then_inc(mix_lo_ready, 2)
                factor(0)
                factor(1)
                low_pair(n + 12)
                low(0)
                low(1)
                factor(2)
                scale_o(3)
                factor(3)
                low_pair(n + 13)
                low(2)
                low_pair(n + 14)
                low(3)
                mix_tail(0)

            def mix_tail(layer):
                n = wout_base(layer)
                low_pair(n + 3)
                low_pair(n + 4)
                finish(2 * layer + 1)
                dve.wait_ge(lo_ready, n + 6)
                low_pair(n + 6)
                norm_diag(2 * layer + 1)

            def attention(layer):
                moba = layer == 1
                n0 = mix_base(layer)
                G0 = 0 if moba else GROUPS
                norm_row(2 * layer)
                if moba:
                    link(dve.tensor_tensor(cos_r[:, :], cos_t[:, :], R_sb[:, :], ALU.mult))
                    link(dve.tensor_tensor(sin_r[:, :], sin_t[:, :], R_sb[:, :], ALU.mult))

                def rotate1(g, j):
                    scale = DH ** -0.5 if j == 0 else 1.0
                    if moba:
                        dve.wait_ge(qk_raw_ready, 2 * g + j + 1)
                        dve.tensor_tensor(qk_lo[:, j], flat(j), qk_hi[:, j].bitcast(F32), ALU.subtract)
                        dve.scalar_tensor_tensor(out=rot1[:, j], in0=flat(j), scalar=scale,
                                                 in1=bcast(cos_r[:, :], 2), op0=ALU.mult, op1=ALU.mult)\
                           .then_inc(qk_lo_ready, 1)
                    else:
                        dve.wait_ge(pair_used, n0 + j + 1 + 3 * g)
                        dve.scalar_tensor_tensor(out=(q_f, k_f)[j][:, :, :], in0=flat(j), scalar=scale,
                                                 in1=bcast(R_sb[:, :], 2), op0=ALU.mult, op1=ALU.mult)\
                           .then_inc(qk_ready, 1)

                def rotate2(g, j):
                    if moba:
                        dve.wait_ge(perm_done, 2 * g + j + 1)
                        dve.scalar_tensor_tensor(out=rot2[:, j], in0=flat(j), scalar=DH ** -0.5 if j == 0 else 1.0,
                                                 in1=bcast(sin_r[:, :], 2), op0=ALU.mult, op1=ALU.mult)\
                           .then_inc(rot_turned, 1)
                        dve.wait_ge(rot_turned, 2 * g + j + 1)
                        dve.tensor_tensor((q_f, k_f)[j][:, :, :], rot1[:, j], rot2[:, j], ALU.add)\
                           .then_inc(qk_ready, 1)

                def soft1(g, banks=(2, 4)):
                    for half in range(2):
                        hs = slice(2 * half, 2 * half + 2)
                        if moba:
                            dve.wait_ge(scores_done, 2 * g + half + 1)
                            c, b = 4 * half, banks[half]
                            dve.tensor_reduce(mx[:, c:c + 2], ps[:, b:b + 2, 0:P], AX.X, ALU.max)
                            dve.tensor_reduce(mx[:, c + 2:c + 4], ps[:, b:b + 2, P:384], AX.X, ALU.max)\
                               .then_inc(softmax_step, 1)
                            dve.wait_ge(softmax_step, 4 * g + half + 1)
                            dve.tensor_scalar(nmx[:, c:c + 4], mx[:, c:c + 4], -1.0, None, ALU.mult).then_inc(nmax_ready, 1)
                        else:
                            dve.wait_ge(log_ready, 2 * g + half + 1)
                            dve.scalar_tensor_tensor(out=prob[:, hs, :], in0=ps[:, banks[half]:banks[half] + 2, 0:384],
                                                     scalar=0.0, in1=sp_a[:, hs, :], op0=ALU.max, op1=ALU.add)\
                               .then_inc(soft_ready, 1)
                    if not moba:
                        for half in range(2):
                            hs = slice(2 * half, 2 * half + 2)
                            dve.wait_ge(soft_hi_ready, 2 * g + half + 1)
                            dve.tensor_tensor(soft_lo[:, hs, :], prob[:, hs, :], soft_hi[:, hs, :].bitcast(F32), ALU.subtract)\
                               .then_inc(prob_ready, 1)
                    else:
                        for half in range(2):
                            hs = slice(2 * half, 2 * half + 2)
                            c = 4 * half
                            dve.wait_ge(exp_done, 2 * g + half + 1)
                            dve.reciprocal(rinv[:, c:c + 4], rsum[:, c:c + 4]).then_inc(softmax_step, 1)
                            dve.wait_ge(softmax_step, 4 * g + 3 + half)
                            for (a, b), cc in (((0, P), c), ((P, 384), c + 2)):
                                last = dve.tensor_tensor(prob[:, hs, a:b], prob[:, hs, a:b],
                                                         rinv[:, cc:cc + 2].unsqueeze(2).to_broadcast([P, 2, b - a]), ALU.mult)
                            last.then_inc(prob_ready, 1)

                def soft2(g, banks=(2, 4)):
                    if moba:
                        dve.wait_ge(stage2_done, 2 * g + 1)
                        dve.tensor_copy(prob_t[:, 0:2, :], ps[:, banks[0]:banks[0] + 2, 0:384]).then_inc(probt_dve, 1)

                def mixed(g, bank=NORM):
                    dve.wait_ge(mix_hi_ready, 2 * g + C * layer + 2)
                    a, b = ((m[:, bass.ds(2 * g, 2), :] if not isinstance(g, int) else m[:, 2 * g:2 * g + 2, :])
                            for m in (mix_lo, mix_hi))
                    dve.tensor_tensor(a, flat(bank), b.bitcast(F32), ALU.subtract).then_inc(mix_lo_ready, 2)

                rotate1(0, 0)
                rotate1(0, 1)
                rotate2(0, 0)
                rotate2(0, 1)
                low_pair(n0 + 3)
                low_pair(n0 + 4)
                with dve.Fori(0, GROUPS - 1) as g:
                    soft1(g)
                    low_pair(n0 + 5, g)
                    rotate1(g + 1, 0)
                    soft2(g)
                    low_pair(n0 + 6, g)
                    rotate1(g + 1, 1)
                    rotate2(g + 1, 0)
                    mixed(g)
                    rotate2(g + 1, 1)
                    low_pair(n0 + 7, g)
                soft1(GROUPS - 1, LAST_BANKS)
                low_pair(n0 + 14)
                soft2(GROUPS - 1, LAST_BANKS)
                mixed(GROUPS - 1, 0)
                mix_tail(layer)

            def conv():
                n0 = mix_base(2)
                norm_row(4)

                def body(c, first):
                    g = c - 1 if not first else 0
                    base = 3 if first else 6

                    def evac(part, dst, bank):
                        dve.wait_ge(pair_used, n0 + part + 1 + 3 * c)
                        dve.tensor_tensor(dst[:, :, :], flat(bank), bcast(R_sb[:, :], 2), ALU.mult).then_inc(conv_evac, 1)
                        low_pair(n0 + base + part, g)
                    evac(0, b_sc, SPARE)
                    evac(1, c_sc, 0)
                    evac(2, cu_sc, 1)
                    for tap in (1, 0):
                        for j in range(2):
                            if tap == 1:
                                dve.wait_ge(y_act, 2 * c + j + 1)
                            else:
                                dve.wait_ge(y_ready, 4 * c + j + 1)
                            col = ROW_CONV + 8 * tap + j
                            w = cols[:, col:col + 1] if first else cols[:, bass.ds(2 * c + col, 1)]
                            dve.scalar_tensor_tensor(out=y_sb[:, j, :], in0=z_pad[:, j, tap:tap + T], scalar=w,
                                                     in1=y_sb[:, j, :], op0=ALU.mult, op1=ALU.add).then_inc(y_ready, 1)
                    dve.wait_ge(mix_hi_ready, C * 2 + 2 * c + 2)
                    lo, hi = ((m[:, 0:2, :] if first else m[:, bass.ds(2 * c, 2), :]) for m in (mix_lo, mix_hi))
                    dve.tensor_tensor(lo, mix32[:, 0], hi.bitcast(F32), ALU.subtract).then_inc(mix_lo_ready, 2)
                body(0, True)
                with dve.Fori(1, GROUPS) as c:
                    body(c, False)
                mix_tail(2)

            def ffn(layer):
                n = ffn_base(layer)
                t0 = FP * layer
                norm_row(2 * layer + 1)

                def scale(dst, signal, pair, bank):
                    dve.wait_ge(pair_used, pair + 1)
                    dve.tensor_tensor(dst[:, :, :], flat(bank), bcast(R_sb[:, :], 2), ALU.mult).then_inc(signal, 1)

                def ups(pair, t, set_, between=None):
                    scale(u_sc, u_scaled, pair, 1)
                    dve.wait_ge(silu_done, t + 1)
                    dve.wait_ge(u_scaled, t + 1)
                    dve.tensor_tensor(hid[:, :, :], sil[:, :, :], u_sc[:, :, :], ALU.mult).then_inc(hid_ready, 1)
                    if between is not None:
                        between()
                    dve.wait_ge(h_hi_ready, t + 1)
                    dve.tensor_tensor(h_lo[:, set_], hid[:, :, :], h_hi[:, set_].bitcast(F32), ALU.subtract)\
                       .then_inc(h_lo_ready, 1)

                scale(g_sc, g_scaled, n, 0)
                ups(n + 1, t0, 0, between=lambda: low_pair(n + 3))
                low_pair(n + 4)
                if layer == 0:
                    trig_tables()
                with dve.Fori(0, FP - 2) as i:
                    scale(g_sc, g_scaled, 3 * i + (n + 2), 0)
                    low_pair(n + 5, i)
                    low_pair(n + 6, i)
                    ups(3 * i + (n + 4), i + t0 + 1, 0)
                    low_pair(n + 7, i)
                t, m = t0 + FP - 1, n + 3 * FP
                scale(g_sc, g_scaled, m - 4, 0)
                low_pair(m - 1)
                ups(m - 3, t, 1)
                low_pair(m)
                if layer < LAYERS - 1:
                    finish(2 * layer + 2)
                    dve.wait_ge(lo_ready, m + 2)
                    low_pair(m + 2)
                    norm_diag(2 * layer + 2)

            for layer in range(LAYERS):
                if layer == 0:
                    mlstm()
                elif layer == 2:
                    conv()
                else:
                    attention(layer)
                ffn(layer)
            def gained(half, tt):
                dve.wait_ge(fin_ps, half + 1)
                if tt == 0:
                    dve.wait_ge(fin_squared, 2 * half + 1)
                part = slice(half * 512, (half + 1) * 512)
                dve.tensor_tensor(xtok[:, tt, part], ps[:, FINAL_BANKS[tt][half], :], final_b[:, part], ALU.mult)\
                   .then_inc(fin_gained, 1)

            for b in range(3):
                residual(8, b)
            dve.wait_ge(fin_landed, 16)
            gained(0, 1)
            residual(8, 3)
            gained(0, 0)
            gained(1, 1)
            gained(1, 0)
            dve.wait_ge(fin_squared, 2 * TT)
            dve.tensor_tensor(fin_sums[:, 0, :], fin_sums[:, 0, :], fin_sums[:, 1, :], ALU.add).then_inc(fin_summed, 1)
            dve.wait_ge(sd_ready, 2 * LAYERS + 1)
            dve.reciprocal(rms_col[:, :], rms_sd[:, :]).then_inc(fin_rms, 1)
            dve.wait_ge(fin_rms, 1)
            for part in (slice(0, 512), slice(512, D)):
                dve.tensor_scalar(xtok[:, 1, part], xtok[:, 1, part], rms_col[:, 1:2], None, ALU.mult)\
                   .then_inc(fin_ready[1], 1)

        @block_ctx.gpsimd
        def _(pool):
            pool.memset(ident, 0.0).then_inc(pool_cleared, 1)
            pool.wait_ge(pool_cleared, 1)
            pool.affine_select(out=ident, in_=ident, compare_op=ALU.not_equal, fill=1.0, base=0,
                               pattern=[[-1, P]], channel_multiplier=1).then_inc(ident_set, 1)
            pool.memset(gate_hi[:, :, :].bitcast(F32), 0.0)
            pool.memset(gate_lo[:, :, :].bitcast(F32), 0.0).then_inc(gw_zero, 1)
            pool.memset(z_pad[:, :, 0:2], 0.0)
            pool.memset(kbf[:, :, :], 0.0)
            pool.memset(suffix_raw, 0.0).then_inc(pool_cleared, 1)
            pool.wait_ge(pool_cleared, 2)
            for dst, compare, fill, base, sign in (
                    (kbf[:, B_IDENT, :], ALU.not_equal, 1.0, 0, 1),
                    (kbf[:, B_MASK_TS, :], ALU.is_ge, NEG, 0, 1),
                    (kbf[:, B_MASK_ST, :], ALU.is_ge, NEG, 0, -1),
                    (kbf[:, B_STRICT_ST, :], ALU.is_gt, NEG, 0, -1),
                    (suffix_raw, ALU.is_gt, -1.0, 0, -1)):
                pool.affine_select(out=dst, in_=dst, compare_op=compare, fill=fill, base=base,
                                   pattern=[[-sign, P]], channel_multiplier=sign).then_inc(kbf_ready, 1)

            def low_pair(n):
                slot = n % SLOTS
                pool.wait_ge(hi_ready, n + 1)
                pool.wait_ge(lo_ready, n)
                pool.tensor_tensor(w_lo[:, slot, :], w_raw[:, slot, :], w_hi[:, slot, :].bitcast(F32), ALU.subtract)\
                    .then_inc(lo_ready, 1)

            def sum_squares(block):
                rr = resid[:, 4:6, :]
                pool.wait_ge(resid_ready, 4 * block + 3)
                if block > 0:
                    pool.wait_ge(ss_col, block)
                pool.tensor_tensor(ss[:, :, :], rr, rr, ALU.mult).then_inc(ss_added, 1)
                pool.wait_ge(ss_added, 2 * block + 1)
                pool.wait_ge(sq_ready, 2 * block + 1)
                pool.tensor_tensor(ss[:, :, :], ss[:, :, :], sq[:, 0], ALU.add).then_inc(ss_added, 1)
                pool.wait_ge(ss_added, 2 * block + 2)
                pool.wait_ge(last_squared, block + 1)
                pool.tensor_tensor(ss[:, :, :], ss[:, :, :], sq[:, 1], ALU.add).then_inc(ss_complete, 1)

            sum_squares(0)
            for h in range(MH):
                pool.wait_ge(num_ready, h + 1)
                if h >= 1:
                    pool.wait_ge(m_s3, h)
                pool.tensor_tensor(nsq[:, :, :], nums[:, h], nums[:, h], ALU.mult).then_inc(nsq_ready, 1)
            for h in range(MH):
                pool.wait_ge(m_t_ready, h + 1)
                pool.wait_ge(o_sig, h + 1)
                if h >= 2:
                    pool.wait_ge(mix_lo_ready, 2 * h - 2)
                pool.tensor_tensor(mix32[:, h % 2], mlt[:, h % 2], o_sc[:, 2 * h:2 * h + 2, :], ALU.mult).then_inc(m_mix, 1)
            for block in range(1, 5):
                low_pair(second_of(block))
                sum_squares(block)
            with pool.Fori(0, GROUPS) as c:
                pool.wait_ge(conv_evac, 3 * c + 3)
                pool.tensor_tensor(z_pad[:, :, 2:T + 2], c_sc[:, :, :], cu_sc[:, :, :], ALU.mult).then_inc(z_ready, 1)
                pool.wait_ge(y_ready, 4 * c + 4)
                pool.tensor_tensor(mix32[:, 0], y_sb[:, :, :], b_sc[:, :, :], ALU.mult).then_inc(cmix_ready, 1)
            for block in range(5, 8):
                low_pair(second_of(block))
                sum_squares(block)


_INS = ["x", "positions", "norm_gains", "mlstm_w_in", "mlstm_b_gate", "mlstm_head_gain", "mlstm_w_out",
        "moba_w_qkv", "moba_w_out", "conv_w_in", "conv_w", "conv_w_out", "sb_w_qkv", "sb_w_out",
        "ffn_w_gate", "ffn_w_up", "ffn_w_down", "final_gain"]


def kernel(**inputs):
    import numpy as _np
    import concourse.bacc as _bacc
    from concourse import mybir as _mybir
    from concourse.bass_utils import run_bass_kernel_spmd as _run

    nc = _bacc.Bacc("TRN2", target_bir_lowering=False, num_devices=1)
    arrays, args = {}, []
    constants, rope_rows = shape_constants()
    given = {name: _np.ascontiguousarray(inputs[name]) for name in _INS}
    given["perm_const"], given["rope_rows"] = constants, rope_rows
    for name, a in given.items():
        arrays[f"in_{name}"] = a
        args.append(nc.dram_tensor(f"in_{name}", a.shape, _mybir.dt.from_np(a.dtype), kind="ExternalInput").ap())
    args.append(nc.dram_tensor("out_0", (1, T, D), _mybir.dt.float32, kind="ExternalOutput").ap())
    build(nc, *args)
    r = _run(nc, [arrays], core_ids=[0])
    return r.results[0]["out_0"]
```
